# Optimizing a Trainium2 kernel written in Bass

```python
import math
import jax, jax.numpy as jnp
from jax import lax
import numpy as np

D_MODEL = 1024
BATCH = 1
SEQ = 512
DEPTH = 2

GRID_W = 64
CTX_LEN = 256
HEAD_DIM = 64
QBLK = 128
ROPE_THETA = 10000.0
EPS = 1e-6
NEG_INF = -1e30

A_HEADS = 8
A_KV_HEADS = 2
B_HEADS = 8
B_KV_HEADS = 2
B_WINDOW = 128
AB_SIZES = (A_HEADS * HEAD_DIM, A_KV_HEADS * HEAD_DIM, A_KV_HEADS * HEAD_DIM,
            B_HEADS * HEAD_DIM, B_KV_HEADS * HEAD_DIM, B_KV_HEADS * HEAD_DIM)
AB_HEADS = (A_HEADS, A_KV_HEADS, A_KV_HEADS, B_HEADS, B_KV_HEADS, B_KV_HEADS)
AB_SPLITS = (512, 640, 768, 1280, 1408)
AB_IN = 1536
AB_OUT = (A_HEADS + B_HEADS) * HEAD_DIM

C_HEADS = 8
C_V_DIM = 2 * HEAD_DIM
C_QK_WIDTH = C_HEADS * 2 * HEAD_DIM
C_IN = 2 * C_QK_WIDTH + C_HEADS * C_V_DIM
C_OUT = C_HEADS * C_V_DIM

N_EXPERTS = 64
TOP_K = 8
N_GROUPS = 8
TOPK_GROUPS = 4
EXPERT_HIDDEN = 256
SHARED_HIDDEN = 256
ROUTED_SCALE = 2.5
EBLK = 128

N_EVEN = (DEPTH + 1) // 2
N_ODD = DEPTH // 2

kernel_name = "hybrid_dit_gqa_window_diffattn_moe"

def rms_norm(x, g):
    xf = x.astype(jnp.float32)
    y = xf * lax.rsqrt(jnp.mean(xf * xf, axis=-1, keepdims=True) + EPS)
    return y.astype(x.dtype) * g

def modulate(h, shift, scale):
    return h * (1 + scale) + shift

def axial_rope(rows, dtype):
    r = jnp.repeat(jnp.arange(rows, dtype=jnp.float32), GRID_W)
    col = jnp.tile(jnp.arange(GRID_W, dtype=jnp.float32), rows)
    n_pair = HEAD_DIM // 4
    inv = ROPE_THETA ** (-jnp.arange(n_pair, dtype=jnp.float32) / n_pair)
    ang = jnp.concatenate([r[:, None] * inv, col[:, None] * inv], axis=-1)
    return jnp.cos(ang).astype(dtype), jnp.sin(ang).astype(dtype)

def apply_rope(x, cos, sin):
    x1, x2 = x[..., 0::2], x[..., 1::2]
    c = cos[None, :, None, :]
    s = sin[None, :, None, :]
    return jnp.stack([x1 * c - x2 * s, x1 * s + x2 * c], axis=-1).reshape(x.shape)

def sweep_query_blocks(fn, q):
    b, n = q.shape[:2]
    nb = n // QBLK
    qb = q.reshape((b, nb, QBLK) + q.shape[2:]).swapaxes(0, 1)
    o = lax.map(fn, qb)
    return o.swapaxes(0, 1).reshape((b, n) + o.shape[3:])

def gqa_attend(q, k, v, sink=None, mask=None):
    b, nq, hq, d = q.shape
    hkv = k.shape[2]
    qg = q.reshape(b, nq, hkv, hq // hkv, d)
    s = jnp.einsum('bqhgd,bkhd->bhgqk', qg, k, preferred_element_type=jnp.float32) * (d ** -0.5)
    if mask is not None:
        s = jnp.where(mask, s, NEG_INF)
    if sink is not None:
        sk = jnp.broadcast_to(sink.astype(jnp.float32).reshape(hkv, hq // hkv)[None, :, :, None, None],
                              s.shape[:-1] + (1,))
        p = jax.nn.softmax(jnp.concatenate([s, sk], axis=-1), axis=-1)[..., :-1]
    else:
        p = jax.nn.softmax(s, axis=-1)
    o = jnp.einsum('bhgqk,bkhd->bqhgd', p.astype(v.dtype), v)
    return o.reshape(b, nq, hq * d)

def gqa_window_blocks(q, k, v, k_ctx, v_ctx, sink):
    b, n, hq, d = q.shape
    nb = n // QBLK
    lc = k_ctx.shape[1]
    pad = ((0, 0), (QBLK, QBLK), (0, 0), (0, 0))
    kp = jnp.pad(k, pad)
    vp = jnp.pad(v, pad)

    def one(i):
        q0 = i * QBLK
        qblk = lax.dynamic_slice_in_dim(q, q0, QBLK, axis=1)
        kb = lax.dynamic_slice_in_dim(kp, q0, 3 * QBLK, axis=1)
        vb = lax.dynamic_slice_in_dim(vp, q0, 3 * QBLK, axis=1)
        qpos = q0 + jnp.arange(QBLK)
        kpos = q0 - QBLK + jnp.arange(3 * QBLK)
        ok = (jnp.abs(qpos[:, None] - kpos[None, :]) <= B_WINDOW) & (kpos[None, :] >= 0) & (kpos[None, :] < n)
        mask = jnp.concatenate([jnp.ones((QBLK, lc), bool), ok], axis=1)
        return gqa_attend(qblk, jnp.concatenate([k_ctx, kb], axis=1),
                          jnp.concatenate([v_ctx, vb], axis=1), sink=sink, mask=mask)

    o = lax.map(one, jnp.arange(nb))
    return o.swapaxes(0, 1).reshape(b, n, hq * d)

def diff_attend(q, k, v, lam):
    d = q.shape[-1]
    s = jnp.einsum('bqhmd,bkhmd->bhmqk', q, k, preferred_element_type=jnp.float32) * (d ** -0.5)
    p = jax.nn.softmax(s, axis=-1)
    a = p[:, :, 0] - lam * p[:, :, 1]
    return jnp.einsum('bhqk,bkhe->bqhe', a.astype(v.dtype), v)

def mixer_ab(h_lat, h_ctx, w_in, w_out, q_norm, k_norm, sink, cos, sin, want_ctx):
    def project(h):
        b, n, _ = h.shape
        parts = jnp.split(h @ w_in, list(AB_SPLITS), axis=-1)
        qa, ka, va, qb, kb, vb = [p.reshape(b, n, hh, HEAD_DIM) for p, hh in zip(parts, AB_HEADS)]
        return rms_norm(qa, q_norm), rms_norm(ka, k_norm), va, qb, kb, vb

    qa, ka, va, qb, kb, vb = project(h_lat)
    qa, ka = apply_rope(qa, cos, sin), apply_rope(ka, cos, sin)
    qb, kb = apply_rope(qb, cos, sin), apply_rope(kb, cos, sin)
    qa_c, ka_c, va_c, qb_c, kb_c, vb_c = project(h_ctx)

    ka_all = jnp.concatenate([ka_c, ka], axis=1)
    va_all = jnp.concatenate([va_c, va], axis=1)
    oa = sweep_query_blocks(lambda qq: gqa_attend(qq, ka_all, va_all), qa)
    ob = gqa_window_blocks(qb, kb, vb, kb_c, vb_c, sink)
    o_lat = jnp.concatenate([oa, ob], axis=-1) @ w_out
    if want_ctx:
        oa_c = gqa_attend(qa_c, ka_c, va_c)
        ob_c = gqa_attend(qb_c, kb_c, vb_c, sink=sink)
        o_ctx = jnp.concatenate([oa_c, ob_c], axis=-1) @ w_out
    else:
        o_ctx = None
    return o_lat, o_ctx

def mixer_c(h_lat, h_ctx, w_in, w_out, lam_p, subln_g, cos, sin, lambda_init, want_ctx):
    def project(h):
        b, n, _ = h.shape
        q, k, v = jnp.split(h @ w_in, [C_QK_WIDTH, 2 * C_QK_WIDTH], axis=-1)
        return (q.reshape(b, n, C_HEADS, 2, HEAD_DIM), k.reshape(b, n, C_HEADS, 2, HEAD_DIM),
                v.reshape(b, n, C_HEADS, C_V_DIM))

    def rope2(t):
        b, n = t.shape[:2]
        return apply_rope(t.reshape(b, n, C_HEADS * 2, HEAD_DIM), cos, sin).reshape(t.shape)

    def finish(o):
        b, n = o.shape[:2]
        return (rms_norm(o, subln_g) * (1 - lambda_init)).reshape(b, n, C_OUT) @ w_out

    q, k, v = project(h_lat)
    q, k = rope2(q), rope2(k)
    qc, kc, vc = project(h_ctx)
    lp = lam_p.astype(jnp.float32)
    lam = jnp.exp(jnp.sum(lp[0] * lp[1])) - jnp.exp(jnp.sum(lp[2] * lp[3])) + lambda_init
    k_all = jnp.concatenate([kc, k], axis=1)
    v_all = jnp.concatenate([vc, v], axis=1)
    o_lat = finish(sweep_query_blocks(lambda qq: diff_attend(qq, k_all, v_all, lam), q))
    o_ctx = finish(diff_attend(qc, kc, vc, lam)) if want_ctx else None
    return o_lat, o_ctx

def moe(xt, router_w, router_bias, w1, w3, w2, sw1, sw3, sw2):
    t, d = xt.shape
    scores = jax.nn.sigmoid(xt.astype(jnp.float32) @ router_w.astype(jnp.float32))
    sel = scores + router_bias.astype(jnp.float32)
    group_score = lax.top_k(sel.reshape(t, N_GROUPS, N_EXPERTS // N_GROUPS), 2)[0].sum(-1)
    _, gidx = lax.top_k(group_score, TOPK_GROUPS)
    gmask = jax.nn.one_hot(gidx, N_GROUPS, dtype=jnp.float32).sum(1) > 0
    emask = jnp.repeat(gmask, N_EXPERTS // N_GROUPS, axis=1)
    _, idx = lax.top_k(jnp.where(emask, sel, NEG_INF), TOP_K)
    wts = jnp.take_along_axis(scores, idx, axis=1)
    wts = wts / jnp.sum(wts, axis=-1, keepdims=True) * ROUTED_SCALE

    flat_e = idx.reshape(-1)
    order = jnp.argsort(flat_e)
    sorted_e = flat_e[order]
    sorted_tok = order // TOP_K
    sorted_w = wts.reshape(-1)[order]
    counts = jnp.bincount(flat_e, length=N_EXPERTS)
    padded = (counts + EBLK - 1) // EBLK * EBLK
    pad_end = jnp.cumsum(padded)
    pad_start = pad_end - padded
    start = jnp.cumsum(counts) - counts
    dest = pad_start[sorted_e] + jnp.arange(t * TOP_K) - start[sorted_e]
    n_blocks = -(-(t * TOP_K) // EBLK) + N_EXPERTS
    n_slots = n_blocks * EBLK
    slot_tok = jnp.full((n_slots,), t, jnp.int32).at[dest].set(sorted_tok.astype(jnp.int32))
    slot_w = jnp.zeros((n_slots,), xt.dtype).at[dest].set(sorted_w.astype(xt.dtype))
    block_e = jnp.minimum(jnp.searchsorted(pad_end, jnp.arange(n_blocks) * EBLK, side='right'),
                          N_EXPERTS - 1)
    xpad = jnp.concatenate([xt, jnp.zeros((1, d), xt.dtype)], axis=0)

    def expert_block(args):
        tok, e = args
        xb = xpad[tok]
        h = jax.nn.silu(xb @ w1[e]) * (xb @ w3[e])
        return h @ w2[e]

    yb = lax.map(expert_block, (slot_tok.reshape(n_blocks, EBLK), block_e))
    routed = jnp.zeros((t + 1, d), xt.dtype).at[slot_tok].add(yb.reshape(n_slots, d) * slot_w[:, None])[:t]
    shared = (jax.nn.silu(xt @ sw1) * (xt @ sw3)) @ sw2
    return routed + shared

def setup_inputs(seed: int = 0) -> dict:
    key = jax.random.key(seed)
    ks = jax.random.split(key, 26)
    f32 = jnp.float32

    def nrm(k, shape, fan_in, gain=1.0):
        return jax.random.normal(k, shape, f32) * (gain * fan_in ** -0.5)

    def gain(k, shape):
        return 1.0 + 0.05 * jax.random.normal(k, shape, f32)

    return {
        "x": jax.random.normal(ks[0], (BATCH, SEQ, D_MODEL), f32),
        "c": jax.random.normal(ks[1], (BATCH, D_MODEL), f32),
        "ctx": jax.random.normal(ks[2], (BATCH, CTX_LEN, D_MODEL), f32),
        "c_ctx": jax.random.normal(ks[3], (D_MODEL,), f32),
        "ada_w": nrm(ks[4], (DEPTH, D_MODEL, 6 * D_MODEL), D_MODEL, 0.5),
        "ada_b": 0.02 * jax.random.normal(ks[5], (DEPTH, 6 * D_MODEL), f32),
        "norm_g": gain(ks[6], (DEPTH, 4, D_MODEL)),
        "ab_w_in": nrm(ks[7], (N_EVEN, D_MODEL, AB_IN), D_MODEL),
        "ab_w_out": nrm(ks[8], (N_EVEN, AB_OUT, D_MODEL), AB_OUT),
        "a_q_norm": gain(ks[9], (N_EVEN, HEAD_DIM)),
        "a_k_norm": gain(ks[10], (N_EVEN, HEAD_DIM)),
        "b_sink": 0.5 * jax.random.normal(ks[11], (N_EVEN, B_HEADS), f32),
        "c_w_in": nrm(ks[12], (N_ODD, D_MODEL, C_IN), D_MODEL),
        "c_w_out": nrm(ks[13], (N_ODD, C_OUT, D_MODEL), C_OUT),
        "c_lambda": 0.1 * jax.random.normal(ks[14], (N_ODD, 4, HEAD_DIM), f32),
        "c_subln_g": gain(ks[15], (N_ODD, C_V_DIM)),
        "router_w": nrm(ks[16], (DEPTH, D_MODEL, N_EXPERTS), D_MODEL),
        "router_bias": 0.01 * jax.random.normal(ks[17], (DEPTH, N_EXPERTS), f32),
        "exp_w1": nrm(ks[18], (DEPTH, N_EXPERTS, D_MODEL, EXPERT_HIDDEN), D_MODEL),
        "exp_w3": nrm(ks[19], (DEPTH, N_EXPERTS, D_MODEL, EXPERT_HIDDEN), D_MODEL),
        "exp_w2": nrm(ks[20], (DEPTH, N_EXPERTS, EXPERT_HIDDEN, D_MODEL), EXPERT_HIDDEN),
        "sh_w1": nrm(ks[21], (DEPTH, D_MODEL, SHARED_HIDDEN), D_MODEL),
        "sh_w3": nrm(ks[22], (DEPTH, D_MODEL, SHARED_HIDDEN), D_MODEL),
        "sh_w2": nrm(ks[23], (DEPTH, SHARED_HIDDEN, D_MODEL), SHARED_HIDDEN),
    }

def reference(x, c, ctx, c_ctx, ada_w, ada_b, norm_g, ab_w_in, ab_w_out, a_q_norm, a_k_norm, b_sink,
              c_w_in, c_w_out, c_lambda, c_subln_g, router_w, router_bias, exp_w1, exp_w3, exp_w2,
              sh_w1, sh_w3, sh_w2):
    b, n, d = x.shape
    rows = n // GRID_W
    cos, sin = axial_rope(rows, x.dtype)
    sc = jax.nn.silu(c)
    scc = jax.nn.silu(c_ctx)
    x_lat, x_ctx = x, ctx
    lc = ctx.shape[1]

    for l in range(DEPTH):
        last = l == DEPTH - 1
        mod = sc @ ada_w[l] + ada_b[l]
        mod_c = scc @ ada_w[l] + ada_b[l]
        sh1, s1, g1, sh2, s2, g2 = jnp.split(mod[:, None, :], 6, axis=-1)
        csh1, cs1, cg1, csh2, cs2, cg2 = jnp.split(mod_c, 6, axis=-1)

        h_lat = modulate(rms_norm(x_lat, norm_g[l, 0]), sh1, s1)
        h_ctx = modulate(rms_norm(x_ctx, norm_g[l, 0]), csh1, cs1)
        j = l // 2
        if l % 2 == 0:
            o_lat, o_ctx = mixer_ab(h_lat, h_ctx, ab_w_in[j], ab_w_out[j], a_q_norm[j], a_k_norm[j],
                                    b_sink[j], cos, sin, not last)
        else:
            lambda_init = 0.8 - 0.6 * math.exp(-0.3 * l)
            o_lat, o_ctx = mixer_c(h_lat, h_ctx, c_w_in[j], c_w_out[j], c_lambda[j], c_subln_g[j],
                                   cos, sin, lambda_init, not last)
        x_lat = x_lat + g1 * rms_norm(o_lat, norm_g[l, 1])
        if not last:
            x_ctx = x_ctx + cg1 * rms_norm(o_ctx, norm_g[l, 1])

        h_lat = modulate(rms_norm(x_lat, norm_g[l, 2]), sh2, s2).reshape(b * n, d)
        if not last:
            h_ctx = modulate(rms_norm(x_ctx, norm_g[l, 2]), csh2, cs2).reshape(b * lc, d)
            y = moe(jnp.concatenate([h_ctx, h_lat], axis=0), router_w[l], router_bias[l], exp_w1[l],
                    exp_w3[l], exp_w2[l], sh_w1[l], sh_w3[l], sh_w2[l])
            y_ctx = y[:b * lc].reshape(b, lc, d)
            y_lat = y[b * lc:].reshape(b, n, d)
            x_ctx = x_ctx + cg2 * rms_norm(y_ctx, norm_g[l, 3])
        else:
            y_lat = moe(h_lat, router_w[l], router_bias[l], exp_w1[l], exp_w3[l], exp_w2[l],
                        sh_w1[l], sh_w3[l], sh_w2[l]).reshape(b, n, d)
        x_lat = x_lat + g2 * rms_norm(y_lat, norm_g[l, 3])

    return x_lat


_drawn_inputs = setup_inputs


def setup_inputs(seed=0):
    import zlib

    import numpy as np

    out = dict(_drawn_inputs(seed))
    spreads = {}
    factors = {'a_q_norm': 2.878, 'a_k_norm': 3.099, 'b_sink': 8.0}
    for name, (base, spread) in spreads.items():
        noise = np.random.default_rng([zlib.crc32(name.encode()), seed]).standard_normal(out[name].shape)
        drawn = base * np.exp(spread * noise) if base else spread * noise
        out[name] = __import__('jax').numpy.asarray(drawn.astype(out[name].dtype))
    for name, factor in factors.items():
        out[name] = (out[name] * factor).astype(out[name].dtype)
    return out
```

```python
import math
from contextlib import ExitStack

import numpy as np

import concourse.bass as bass
from concourse import mybir

F32 = mybir.dt.float32
BF16 = mybir.dt.bfloat16
I32 = mybir.dt.int32
U32 = mybir.dt.uint32
ALU = mybir.AluOpType
ACT = mybir.ActivationFunctionType
AX = mybir.AxisListType

P = 128
D = 1024
KD = D // P
SEQ, CTX = 512, 256
NTOK = SEQ + CTX
NT, CT = NTOK // P, CTX // P
DEPTH = 2
HD = 64
EPS = 1e-6
GRID_W = 64
THETA = 10000.0
WINDOW = 128
AH, GROUPS_KV = 8, 2
SCALE = HD ** -0.5
CH = 8
E, TOPK, NG, TOPG = 64, 8, 8, 4
EG = E // NG
F = 256
KF = F // P
ROUTED_SCALE = 2.5
RING = 3
LAM_INIT = 0.8 - 0.6 * math.exp(-0.3)
KMAX = NTOK // P
NEG = -1e30


def host_constants():
    p = np.arange(P)
    row = np.arange(SEQ)
    inv = (np.float32(THETA) ** (-np.arange(HD // 4, dtype=np.float32) / np.float32(HD // 4))).astype(np.float32)
    ang = np.concatenate([(row // GRID_W).astype(np.float32)[:, None] * inv,
                          (row % GRID_W).astype(np.float32)[:, None] * inv], axis=-1)
    cos, sin = np.cos(ang).astype(np.float32), np.sin(ang).astype(np.float32)
    cos2 = np.repeat(cos, 2, axis=1)
    sin2 = np.stack([-sin, sin], axis=-1).reshape(SEQ, HD)
    rope = np.stack([cos2, sin2], axis=0).reshape(2, SEQ // P, P, HD).transpose(2, 0, 1, 3)
    ident = np.eye(P, dtype=np.float32)
    q, k = p[:, None], p[None, :]
    band = np.stack([np.where(k >= q, 0, NEG), np.where(k <= q, 0, NEG)], axis=1).astype(np.float32)
    before = (p[:, None] < p[None, :]).astype(np.float32)
    upto = np.zeros((P, E), np.float32)
    upto[:E] = (np.arange(E)[:, None] <= np.arange(E)[None, :])
    i, j = np.arange(NG)[:, None], np.arange(NG)[None, :]
    earlier = np.broadcast_to((j < i).astype(np.float32).reshape(1, NG * NG), (P, NG * NG))
    slots = np.broadcast_to(np.arange(P * (KMAX + 1), dtype=np.float32)[None], (P, P * (KMAX + 1)))
    part = np.stack([p, p + 1], axis=1).astype(np.float32)
    return {"k_rope": np.ascontiguousarray(rope), "k_ident": ident, "k_band": band, "k_before": before,
            "k_upto": upto, "k_earlier": np.ascontiguousarray(earlier), "k_slots": np.ascontiguousarray(slots),
            "k_part": part}


def steps(ap):
    return ap.rearrange("(p k) n -> p k n", p=P)


def column(ap, k):
    return ap.rearrange("a (p k) -> a k p", k=KD)[:, k, :]


def bank_place(i, n):
    half = (n + 1) // 2
    return i * P if i < half else 512 + (i - half) * P


def phase_semaphores(nc, ctx, phase):
    used = []

    def sem(name):
        used.append(nc.alloc_semaphore(name=f"{phase}_{name}"))
        return used[-1]

    def clear():
        nc.clear_and_free_semaphores(used)
        nc.all_engine_barrier()

    ctx.callback(clear)
    return sem


class Core:
    pass


def adaln(nc, s, a):
    chunks = DEPTH * 12
    with ExitStack() as ctx:
        sb = lambda n, sh, dt=F32: ctx.enter_context(nc.sbuf_tensor(n, sh, dt))
        sem = phase_semaphores(nc, ctx, "ada")
        cond = sb("cond", [P, 2, KD])
        cexp = sb("cexp", [P, 2, KD])
        cden = sb("cden", [P, 2, KD])
        crec = sb("crec", [P, 2, KD])
        silu = sb("silu", [P, KD, 2])
        bias = sb("ada_bias", [2, DEPTH * 6 * D])
        gains = sb("ada_gains", [2, DEPTH * 4 * D])
        mrow = sb("mrow", [2, 2, D])
        pm = [ctx.enter_context(nc.psum_tensor(f"ada_ps{i}", [P, 512], F32)) for i in range(2)]
        vec_in, ada_in = sem("vec_in"), [sem(f"ada_in{i}") for i in range(RING)]
        cexp_done, silu_step = sem("cexp_done"), sem("silu_step")
        ada_mm, ada_added, row_step, row_ready = sem("ada_mm"), sem("ada_added"), sem("row_step"), sem("row_ready")
        row_out = [sem(f"row_out{i}") for i in range(2)]
        block = ctx.enter_context(nc.Block())

        @block.sync
        def _(sp):
            sp.dma_start(cond[:, 0, :], a["c"].rearrange("o (p k) -> (o p) k", p=P)).then_inc(vec_in, 16)
            sp.dma_start(cond[:, 1, :], a["c_ctx"].rearrange("(p k) -> p k", p=P)).then_inc(vec_in, 16)
            sp.dma_start(bias[:], a["ada_b"].rearrange("l n -> (l n)").partition_broadcast(2)).then_inc(vec_in, 16)
            sp.dma_start(gains[:], a["norm_g"].rearrange("l v d -> (l v d)").partition_broadcast(2)).then_inc(vec_in, 16)
            for n in range(chunks):
                if n >= RING:
                    sp.wait_ge(ada_mm, n - RING + 1)
                sp.dma_start(s.ring[n % RING][:].rearrange("p (k n) -> p k n", k=KD),
                             steps(a["ada_w"][n // 12])[:, :, (n % 12) * 512:(n % 12 + 1) * 512]).then_inc(ada_in[n % RING], 16)

        @block.scalar
        def _(act):
            act.wait_ge(vec_in, 64)
            nc.scalar.activation(cexp[:], cond[:], ACT.Exp, scale=-1.0).then_inc(cexp_done, 1)
            act.dma_start(s.X[:, 0:CT, :], a["ctx"].rearrange("o (t p) d -> p (o t) d", p=P)).then_inc(s.x_in, 16)
            act.dma_start(s.X[:, CT:NT, :], a["x"].rearrange("o (t p) d -> p (o t) d", p=P)).then_inc(s.x_in, 16)
            for v in range(DEPTH * 6):
                act.wait_ge(row_ready, v + 1)
                act.dma_start(s.mod[v // 6, :, v % 6, :], mrow[:, v % 2, :]).then_inc(row_out[v % 2], 16)
            for i in range(2):
                act.wait_ge(row_out[i], 16 * DEPTH * 3)
            act.wait_ge(s.x_in, 32)

        @block.vector
        def _(dve):
            dve.wait_ge(cexp_done, 1)
            nc.vector.tensor_scalar(cden[:], cexp[:], 1.0, None, ALU.add).then_inc(silu_step, 1)
            dve.wait_ge(silu_step, 1)
            nc.vector.reciprocal(crec[:], cden[:]).then_inc(silu_step, 1)
            dve.wait_ge(silu_step, 2)
            nc.vector.tensor_tensor(silu[:].rearrange("p k c -> p c k"), cond[:], crec[:], ALU.mult).then_inc(silu_step, 1)
            changed = 0
            for n in range(chunks):
                v, half = n // 2, n % 2
                l, vec = v // 6, v % 6
                row = mrow[:, v % 2, half * 512:(half + 1) * 512]
                dve.wait_ge(ada_mm, n + 1)
                if half == 0 and v >= 2:
                    dve.wait_ge(row_out[v % 2], 16 * (v // 2))
                add = nc.vector.tensor_tensor(row, pm[n % 2][0:2, :], bias[:, l * 6 * D + vec * D + half * 512:l * 6 * D + vec * D + (half + 1) * 512], ALU.add)
                add.then_inc(ada_added, 1)
                dve.wait_ge(ada_added, n + 1)
                if vec in (1, 2, 4, 5):
                    g = gains[:, (l * 4 + {1: 0, 2: 1, 4: 2, 5: 3}[vec]) * D + half * 512:(l * 4 + {1: 0, 2: 1, 4: 2, 5: 3}[vec]) * D + (half + 1) * 512]
                    one = 1.0 if vec in (1, 4) else 0.0
                    nc.vector.scalar_tensor_tensor(row, row, one, g, ALU.add, ALU.mult).then_inc(row_step, 1)
                    changed += 1
                    dve.wait_ge(row_step, changed)
                if half:
                    dve.sem_inc(row_ready, 1)

        @block.tensor
        def _(pe):
            pe.wait_ge(silu_step, 3)
            for n in range(chunks):
                pe.wait_ge(ada_in[n % RING], 16 * (n // RING + 1))
                if n >= 2:
                    pe.wait_ge(ada_added, n - 1)
                for k in range(KD):
                    mm = nc.tensor.matmul(pm[n % 2][0:2, :], silu[:, k, :], s.ring[n % RING][:, k * 512:(k + 1) * 512],
                                          start=(k == 0), stop=(k == KD - 1))
                mm.then_inc(ada_mm, 1)


def load_modulation(nc, s, eng, l, half, done):
    for cond in range(2):
        eng.dma_start(s.bc[:, cond, :, :], s.mod[l, cond, 3 * half:3 * half + 3, :].partition_broadcast(P)).then_inc(done, 16)


def sections(l):
    if l == 0:
        return [dict(cols=[(0, 512)], tiles=range(NT), kind="q", norm="q", base=0),
                dict(cols=[(768, 1280)], tiles=range(NT), kind="q", norm=None, base=4),
                dict(cols=[(512, 768), (1280, 1536)], tiles=range(NT), kind="kv", norm="k", base=0)]
    return ([dict(cols=[(i * 512, i * 512 + 512)], tiles=range(CT, NT), kind="q", norm=None, base=4 * i) for i in range(2)]
            + [dict(cols=[(D + i * 512, D + i * 512 + 512)], tiles=range(NT), kind="k", norm=None, base=4 * i) for i in range(2)]
            + [dict(cols=[(2 * D + i * 512, 2 * D + i * 512 + 512)], tiles=range(NT), kind="v", norm=None, base=i) for i in range(2)])


def project(nc, s, a, l, qt, kt, v):
    chunks = sections(l)
    items = [(c, t) for c in range(len(chunks)) for t in chunks[c]["tiles"]]
    w_in = steps((a["ab_w_in"] if l == 0 else a["c_w_in"])[0])
    q0 = 0 if l == 0 else CT
    LAG = 2
    with ExitStack() as ctx:
        sb = lambda n, sh, dt=F32: ctx.enter_context(nc.sbuf_tensor(f"{n}_{l}", sh, dt))
        sem = phase_semaphores(nc, ctx, f"project{l}")
        ps = lambda n, w: ctx.enter_context(nc.psum_tensor(f"{n}_{l}", [P, w], F32))
        ident = sb("p_ident", [P, P])
        rope = sb("p_rope", [P, 2, SEQ // P, HD])
        gains = sb("p_gains", [P, 2, HD])
        hrow = [sb(f"hrow{i}", [P, D]) for i in range(2)]
        ssq, mean, logs, rstd = (sb(f"p_{n}", [P, NT]) for n in ("ssq", "mean", "logs", "rstd"))
        proj = [sb(f"proj{i}", [P, 512]) for i in range(2)]
        rot = [sb(f"rot{i}", [P, 512]) for i in range(2)]
        norm = sb("p_norm", [P, 512])
        t1 = sb("p_t1", [P, 512])
        hss, hmean, hlog, hrstd = (sb(f"ph_{n}", [P, 8]) for n in ("ss", "mean", "log", "rstd"))
        psT = [ps(f"psT{i}", 1024) for i in range(2)]
        psP = [ps(f"psP{i}", 512) for i in range(2)]
        psQ = [ps(f"psQ{i}", 512) for i in range(2)]
        w_at = [sem(f"w_in{i}") for i in range(RING)]
        const_in, bc_in = sem("const_in"), sem("bc_in")
        dve_done, mean_ready, rstd_ready = sem("dve_done"), sem("mean_ready"), sem("rstd_ready")
        hrow_ready, t_mm, ht_ready = sem("hrow_ready"), sem("t_mm"), sem("ht_ready")
        p_mm, p_copied, proj_read = sem("p_mm"), sem("p_copied"), sem("proj_read")
        hmean_ready, hrstd_ready = sem("hmean_ready"), sem("hrstd_ready")
        rot_ready, q_mm, q_copied, act_step = sem("rot_ready"), sem("q_mm"), sem("q_copied"), sem("act_step")
        block = ctx.enter_context(nc.Block())
        HT = s.ho[:].rearrange("p (k n) -> p k n", k=KD)
        normed = [i for i, (c, t) in enumerate(items) if chunks[c]["norm"]]

        @block.sync
        def _(sp):
            load_modulation(nc, s, sp, l, 0, bc_in)
            sp.dma_start(ident[:], a["k_ident"]).then_inc(const_in, 16)
            sp.dma_start(rope[:], a["k_rope"]).then_inc(const_in, 16)
            sp.dma_start(gains[:, 0, :], a["a_q_norm"][0].partition_broadcast(P)).then_inc(const_in, 16)
            sp.dma_start(gains[:, 1, :], a["a_k_norm"][0].partition_broadcast(P)).then_inc(const_in, 16)
            for c, ch in enumerate(chunks):
                if c >= RING:
                    sp.wait_ge(p_mm, sum(len(x["tiles"]) for x in chunks[:c - RING + 1]))
                dst = s.ring[c % RING][:].rearrange("p (k n) -> p k n", k=KD)
                at = 0
                for lo, hi in ch["cols"]:
                    sp.dma_start(dst[:, :, at:at + hi - lo], w_in[:, :, lo:hi]).then_inc(w_at[c % RING], 16)
                    at += hi - lo

        def w_need(c):
            return 16 * sum(len(chunks[i]["cols"]) for i in range(c % RING, c + 1, RING))

        @block.vector
        def _(dve):
            chain = [0]

            def link(ins):
                chain[0] += 1
                ins.then_inc(dve_done, 1)
                dve.wait_ge(dve_done, chain[0])

            for t in range(NT):
                link(nc.vector.tensor_tensor_reduce(out=hrow[0][:], in0=s.X[:, t, :], in1=s.X[:, t, :], scale=1.0, scalar=0.0,
                                                    op0=ALU.mult, op1=ALU.add, accum_out=ssq[:, t:t + 1]))
            nc.vector.tensor_scalar(mean[:], ssq[:], 1.0 / D, EPS, ALU.mult, ALU.add).then_inc(mean_ready, 1)
            dve.wait_ge(bc_in, 32)
            dve.wait_ge(rstd_ready, 1)
            for t in range(NT):
                cond = 1 if t < CT else 0
                if t >= 2:
                    dve.wait_ge(t_mm, t - 1)
                link(nc.vector.scalar_tensor_tensor(hrow[t % 2][:], s.X[:, t, :], rstd[:, t:t + 1], s.bc[:, cond, 1, :], ALU.mult, ALU.mult))
                nc.vector.tensor_tensor(hrow[t % 2][:], hrow[t % 2][:], s.bc[:, cond, 0, :], ALU.add).then_inc(hrow_ready, 1)
            dve.wait_ge(const_in, 64)

            def bcast(ap, n):
                return ap.unsqueeze(1).to_broadcast([P, n, HD])

            def head_part(n, t, src, dst, heads, gain):
                flat = src
                if gain is not None:
                    sq = t1[:, 0:heads * HD].rearrange("p (h d) -> p h d", d=HD)
                    link(nc.vector.tensor_tensor(sq, flat, flat, ALU.mult))
                    link(nc.vector.tensor_reduce(hss[:, 0:heads], sq, AX.X, ALU.add))
                    nc.vector.tensor_scalar(hmean[:, 0:heads], hss[:, 0:heads], 1.0 / HD, EPS, ALU.mult, ALU.add).then_inc(hmean_ready, 1)
                    dve.wait_ge(hrstd_ready, normed.index(n) + 1)
                    nv = norm[:, 0:heads * HD].rearrange("p (h d) -> p h d", d=HD)
                    link(nc.vector.tensor_tensor(nv, flat, hrstd[:, 0:heads].unsqueeze(2).to_broadcast([P, heads, HD]), ALU.mult))
                    if t < CT:
                        link(nc.vector.tensor_tensor(dst, regroup(nv, heads), gain4(gain, heads), ALU.mult))
                        return
                    link(nc.vector.tensor_tensor(nv, nv, bcast(gains[:, gain, :], heads), ALU.mult))
                    flat = nv
                elif t < CT:
                    link(nc.vector.tensor_copy(dst, regroup(flat, heads)))
                    return
                cos, sin = rope[:, 0, t - CT, :], rope[:, 1, t - CT, :]
                tv = t1[:, 0:heads * HD].rearrange("p (h d) -> p h d", d=HD)
                tp = tv.rearrange("p h (i e) -> p h i e", e=2)
                fp = flat.rearrange("p h (i e) -> p h i e", e=2)
                sp2 = sin.rearrange("p (i e) -> p i e", e=2)
                for e in range(2):
                    link(nc.vector.tensor_tensor(tp[:, :, :, e], fp[:, :, :, 1 - e],
                                                 sp2[:, :, e].unsqueeze(1).to_broadcast([P, heads, HD // 2]), ALU.mult))
                if flat is src:
                    nv = norm[:, 0:heads * HD].rearrange("p (h d) -> p h d", d=HD)
                link(nc.vector.tensor_tensor(nv, flat, bcast(cos, heads), ALU.mult))
                link(nc.vector.tensor_tensor(dst, regroup(nv, heads), regroup(tv, heads), ALU.add))

            def split(heads):
                return l == 0 and heads == AH

            def regroup(ap, heads):
                return ap.rearrange("p (g j) d -> p g j d", g=GROUPS_KV) if split(heads) else ap

            def gain4(gain, heads):
                g = gains[:, gain, :]
                if split(heads):
                    return g.unsqueeze(1).unsqueeze(1).to_broadcast([P, GROUPS_KV, heads // GROUPS_KV, HD])
                return bcast(g, heads)

            for n, (c, t) in enumerate(items):
                ch = chunks[c]
                if ch["kind"] == "v":
                    continue
                dve.wait_ge(p_copied, n + 1)
                if n >= LAG:
                    dve.wait_ge(q_mm, n - LAG + 1)
                pr = proj[n % 2][:].rearrange("p (h d) -> p h d", d=HD)
                if ch["kind"] == "kv":
                    rt = rot[n % 2][:].rearrange("p (h d) -> p h d", d=HD)
                    head_part(n, t, pr[:, 0:2, :], rt[:, 0:2, :], 2, 1)
                    head_part(n, t, pr[:, 4:6, :], rt[:, 2:4, :], 2, None)
                elif l == 0:
                    head_part(n, t, pr, rot[n % 2][:].rearrange("p (j g d) -> p g j d", g=GROUPS_KV, d=HD), AH, 0 if ch["norm"] else None)
                else:
                    head_part(n, t, pr, rot[n % 2][:].rearrange("p (h d) -> p h d", d=HD), 8, None)
                dve.sem_inc(rot_ready, 1)

        @block.scalar
        def _(act):
            acts = [0]

            def link(ins):
                acts[0] += 1
                ins.then_inc(act_step, 1)
                act.wait_ge(act_step, acts[0])

            act.wait_ge(mean_ready, 1)
            link(nc.scalar.activation(logs[:], mean[:], ACT.Ln))
            nc.scalar.activation(rstd[:], logs[:], ACT.Exp, scale=-0.5).then_inc(rstd_ready, 1)
            for t in range(NT):
                act.wait_ge(t_mm, t + 1)
                nc.scalar.copy(HT[:, :, t * P:(t + 1) * P], psT[t % 2][:].rearrange("p (k n) -> p k n", k=KD)).then_inc(ht_ready, 1)

            def move_out(n):
                c, t = items[n]
                ch = chunks[c]
                if ch["kind"] == "v":
                    return
                act.wait_ge(q_mm, n + 1)
                if ch["kind"] == "kv":
                    out, src = kt[:, 0:2, t * P:(t + 1) * P], psQ[n % 2][:, 0:256]
                elif ch["kind"] == "k":
                    out, src = kt[:, ch["base"]:ch["base"] + 4, t * P:(t + 1) * P], psQ[n % 2][:]
                else:
                    out, src = qt[:, ch["base"]:ch["base"] + 4, (t - q0) * P:(t - q0 + 1) * P], psQ[n % 2][:]
                nc.scalar.copy(out, src.rearrange("p (j n) -> p j n", n=P)).then_inc(q_copied, 1)

            for n, (c, t) in enumerate(items):
                ch = chunks[c]
                act.wait_ge(p_mm, n + 1)
                if ch["kind"] == "v":
                    nc.scalar.copy(v[:, t, ch["base"] * 512:ch["base"] * 512 + 512], psP[n % 2][:]).then_inc(p_copied, 1)
                else:
                    if n >= 2:
                        act.wait_ge(rot_ready, n - 1)
                    if ch["kind"] == "kv":
                        link(nc.scalar.copy(v[:, t, :].rearrange("p (u n) -> p u n", u=2),
                                            psP[n % 2][:].rearrange("p (u w n) -> p u w n", u=2, w=2)[:, :, 1, :]))
                    nc.scalar.copy(proj[n % 2][:], psP[n % 2][:]).then_inc(p_copied, 1)
                if n in normed:
                    h = AH if ch["kind"] == "q" else GROUPS_KV
                    act.wait_ge(hmean_ready, normed.index(n) + 1)
                    link(nc.scalar.activation(hlog[:, 0:h], hmean[:, 0:h], ACT.Ln))
                    nc.scalar.activation(hrstd[:, 0:h], hlog[:, 0:h], ACT.Exp, scale=-0.5).then_inc(hrstd_ready, 1)
                if n >= LAG:
                    move_out(n - LAG)
            for n in range(len(items) - LAG, len(items)):
                move_out(n)

        @block.tensor
        def _(pe):
            pe.wait_ge(const_in, 64)
            for t in range(NT):
                pe.wait_ge(hrow_ready, t + 1)
                if t >= 2:
                    pe.wait_ge(ht_ready, t - 1)
                for k in range(KD):
                    tr = nc.tensor.transpose(psT[t % 2][:, k * P:(k + 1) * P], column(hrow[t % 2][:], k), ident[:])
                tr.then_inc(t_mm, 1)

            def turn(n):
                c, t = items[n]
                kind = chunks[c]["kind"]
                if kind == "v":
                    return
                pe.wait_ge(rot_ready, n + 1)
                if n >= 2:
                    pe.wait_ge(q_copied, n - 1)
                for j in range(2 if kind == "kv" else 4):
                    tr = nc.tensor.transpose(psQ[n % 2][:, j * P:(j + 1) * P], rot[n % 2][:, j * P:(j + 1) * P], ident[:])
                tr.then_inc(q_mm, 1)

            for n, (c, t) in enumerate(items):
                pe.wait_ge(w_at[c % RING], w_need(c))
                pe.wait_ge(ht_ready, min(t + 1, NT))
                if n >= 2:
                    pe.wait_ge(p_copied, n - 1)
                for k in range(KD):
                    mm = nc.tensor.matmul(psP[n % 2][:], HT[:, k, t * P:(t + 1) * P], s.ring[c % RING][:, k * 512:(k + 1) * 512],
                                          start=(k == 0), stop=(k == KD - 1))
                mm.then_inc(p_mm, 1)
                if n >= LAG:
                    turn(n - LAG)
            for n in range(len(items) - LAG, len(items)):
                turn(n)


def prefetch_out(nc, s, a, l, sp):
    w_out = steps((a["ab_w_out"] if l == 0 else a["c_w_out"])[0])
    for c in range(2):
        sp.dma_start(s.ring[c][:].rearrange("p (k n) -> p k n", k=KD), w_out[:, :, c * 512:(c + 1) * 512]).then_inc(s.wo_in[c], 16)


def attend_ab(nc, s, a, qt, kt, v):
    units = []
    for t in range(NT):
        for kind in range(2):
            if t < CT:
                keys = [(i, None) for i in range(CT)]
            elif kind == 0:
                keys = [(i, None) for i in range(NT)]
            else:
                near = [i for i in (t - 1, t, t + 1) if CT <= i < NT]
                keys = [(i, None) for i in range(CT)] + [(i, {-1: 0, 0: None, 1: 1}[i - t]) for i in near]
            for h in range(AH):
                units.append((t, kind, h, keys))

    def pieces(keys):
        out = []
        for i, (k, _) in enumerate(keys):
            if out and out[-1][1] + out[-1][2] == k and i % 4:
                out[-1][2] += 1
            else:
                out.append([i, k, 1])
        return out

    n_units = len(units)
    with ExitStack() as ctx:
        sb = lambda n, sh, dt=F32: ctx.enter_context(nc.sbuf_tensor(n, sh, dt))
        sem = phase_semaphores(nc, ctx, "attend_ab")
        ps = lambda n, w: ctx.enter_context(nc.psum_tensor(n, [P, w], F32))
        ident = sb("a_ident", [P, P])
        band = sb("a_band", [P, 2, P])
        sink = sb("a_sink", [P, AH])
        nsink = sb("a_nsink", [P, AH])
        top = sb("a_top", [P, 2])
        ntop = sb("a_ntop", [P, 2])
        total = sb("a_total", [P, 4])
        esink = sb("a_esink", [P, 4])
        den = sb("a_den", [P, 4])
        inv = sb("a_inv", [P, 4])
        prob = [sb(f"a_prob{i}", [P, NT * P]) for i in range(2)]
        probT = [sb(f"a_probT{i}", [P, NT * P]) for i in range(2)]
        psS = [ps(f"a_psS{i}", 1024) for i in range(2)]
        psT = ps("a_psT", 1024)
        psO = [ps(f"a_psO{i}", 512) for i in range(2)]
        const_in, dve_done = sem("const_in"), sem("dve_done")
        s_mm, top_ready, exp_done = sem("s_mm"), sem("top_ready"), sem("exp_done")
        t_mm, t_copied, o_mm, o_ready, den_ready = sem("t_mm"), sem("t_copied"), sem("o_mm"), sem("o_ready"), sem("den_ready")
        block = ctx.enter_context(nc.Block())
        O = s.ho[:].rearrange("p (t n) -> p t n", t=NT)

        @block.sync
        def _(sp):
            sp.dma_start(ident[:], a["k_ident"]).then_inc(const_in, 16)
            sp.dma_start(band[:], a["k_band"]).then_inc(const_in, 16)
            sp.dma_start(sink[:], a["b_sink"][0].partition_broadcast(P)).then_inc(const_in, 16)
            prefetch_out(nc, s, a, 0, sp)

        @block.tensor
        def _(pe):
            pe.wait_ge(const_in, 48)

            def scores(u):
                t, kind, h, keys = units[u]
                g, j = h // 4, h % 4
                if u >= 2:
                    pe.wait_ge(exp_done, u - 1)
                for at, k0, n in pieces(keys):
                    mm = nc.tensor.matmul(psS[u % 2][:, at * P:(at + n) * P], qt[g * HD:(g + 1) * HD, kind * 4 + j, t * P:(t + 1) * P],
                                          kt[g * HD:(g + 1) * HD, kind, k0 * P:(k0 + n) * P], start=True, stop=True)
                mm.then_inc(s_mm, 1)

            def turn(u):
                pe.wait_ge(exp_done, u + 1)
                if u >= 1:
                    pe.wait_ge(t_copied, 2 * u)
                nk = len(units[u][3])
                for i in range(nk):
                    at = bank_place(i, nk)
                    tr = nc.tensor.transpose(psT[:, at:at + P], prob[u % 2][:, i * P:(i + 1) * P], ident[:])
                tr.then_inc(t_mm, 1)

            def values(u):
                t, kind, h, keys = units[u]
                g = h // 4
                pe.wait_ge(t_copied, 2 * (u + 1))
                if u >= 2:
                    pe.wait_ge(o_ready, u - 1)
                for i, (k, _) in enumerate(keys):
                    mm = nc.tensor.matmul(psO[u % 2][:, 0:HD], probT[u % 2][:, i * P:(i + 1) * P],
                                          v[:, k, kind * P + g * HD:kind * P + (g + 1) * HD], start=(i == 0), stop=(i == len(keys) - 1))
                mm.then_inc(o_mm, 1)

            scores(0)
            for u in range(n_units):
                if u + 1 < n_units:
                    scores(u + 1)
                if u >= 1:
                    values(u - 1)
                turn(u)
            values(n_units - 1)

        @block.vector
        def _(dve):
            chain = [0]

            def link(ins):
                chain[0] += 1
                ins.then_inc(dve_done, 1)
                dve.wait_ge(dve_done, chain[0])

            dve.wait_ge(const_in, 48)
            link(nc.vector.tensor_scalar(nsink[:], sink[:], -1.0, None, ALU.mult))

            def highest(u):
                t, kind, h, keys = units[u]
                dve.wait_ge(s_mm, u + 1)
                for i, (_, edge) in enumerate(keys):
                    if edge is not None:
                        cols = psS[u % 2][:, i * P:(i + 1) * P]
                        link(nc.vector.tensor_tensor(cols, cols, band[:, edge, :], ALU.add))
                b = u % 2
                if u >= 2:
                    dve.wait_ge(den_ready, u - 1)
                link(nc.vector.tensor_reduce(top[:, b:b + 1], psS[b][:, 0:len(keys) * P], AX.X, ALU.max))
                if kind == 1:
                    link(nc.vector.tensor_scalar(ntop[:, b:b + 1], top[:, b:b + 1], -SCALE, nsink[:, h:h + 1], ALU.mult, ALU.min))
                else:
                    link(nc.vector.tensor_scalar(ntop[:, b:b + 1], top[:, b:b + 1], -SCALE, None, ALU.mult))
                dve.sem_inc(top_ready, 1)

            def half_copy(u):
                nk = len(units[u][3])
                n, cut = nk * P, (nk + 1) // 2 * P
                dve.wait_ge(t_mm, u + 1)
                if u >= 2:
                    dve.wait_ge(o_mm, u - 1)
                nc.vector.tensor_copy(probT[u % 2][:, cut:n], psT[:, 512:512 + n - cut]).then_inc(t_copied, 1)

            def finish(u):
                t, kind, h, keys = units[u]
                b = u % 4
                dve.wait_ge(den_ready, u + 1)
                if kind == 1:
                    link(nc.vector.tensor_tensor(den[:, b:b + 1], total[:, b:b + 1], esink[:, b:b + 1], ALU.add))
                    link(nc.vector.reciprocal(inv[:, b:b + 1], den[:, b:b + 1]))
                else:
                    link(nc.vector.reciprocal(inv[:, b:b + 1], total[:, b:b + 1]))
                dve.wait_ge(o_mm, u + 1)
                nc.vector.tensor_scalar(O[:, t, kind * 512 + h * HD:kind * 512 + (h + 1) * HD], psO[u % 2][:, 0:HD],
                                        inv[:, b:b + 1], None, ALU.mult).then_inc(o_ready, 1)

            highest(0)
            for u in range(n_units):
                if u + 1 < n_units:
                    highest(u + 1)
                if u >= 1:
                    finish(u - 1)
                half_copy(u)
            finish(n_units - 1)

        @block.scalar
        def _(act):
            for u in range(n_units):
                t, kind, h, keys = units[u]
                n = len(keys) * P
                b = u % 4
                act.wait_ge(top_ready, u + 1)
                if u >= 2:
                    act.wait_ge(t_mm, u - 1)
                if u >= 4:
                    act.wait_ge(o_ready, u - 3)
                nc.scalar.activation(prob[u % 2][:, 0:n], psS[u % 2][:, 0:n], ACT.Exp, bias=ntop[:, u % 2:u % 2 + 1], scale=SCALE,
                                     accum_out=total[:, b:b + 1]).then_inc(exp_done, 1)
                if kind == 1:
                    nc.scalar.activation(esink[:, b:b + 1], sink[:, h:h + 1], ACT.Exp, bias=ntop[:, u % 2:u % 2 + 1]).then_inc(den_ready, 1)
                else:
                    act.wait_ge(exp_done, u + 1)
                    act.sem_inc(den_ready, 1)
                cut = (len(keys) + 1) // 2 * P
                act.wait_ge(t_mm, u + 1)
                if u >= 2:
                    act.wait_ge(o_mm, u - 1)
                nc.scalar.copy(probT[u % 2][:, 0:cut], psT[:, 0:cut]).then_inc(t_copied, 1)


def attend_c(nc, s, a, qt, kt, v):
    units = [(t, h) for t in range(SEQ // P) for h in range(CH)]
    n_units = len(units)
    NK = NT * P
    with ExitStack() as ctx:
        sb = lambda n, sh, dt=F32: ctx.enter_context(nc.sbuf_tensor(n, sh, dt))
        sem = phase_semaphores(nc, ctx, "attend_c")
        ps = lambda n, w: ctx.enter_context(nc.psum_tensor(n, [P, w], F32))
        ident = sb("c_ident", [P, P])
        lamp = sb("c_lamp", [P, 4, HD])
        lprod = sb("c_lprod", [P, 2, HD])
        lsum, lexp = sb("c_lsum", [P, 2]), sb("c_lexp", [P, 2])
        ldif, nlam = sb("c_ldif", [P, 1]), sb("c_nlam", [P, 1])
        subg = sb("c_subg", [P, P])
        top, ntop = sb("c_top", [P, 2]), sb("c_ntop", [P, 2])
        total, inv, coef = sb("c_total", [P, 2]), sb("c_inv", [P, 2]), sb("c_coef", [P, 1])
        prob = [sb(f"c_prob{m}", [P, NK]) for m in range(2)]
        dif = sb("c_dif", [P, NK])
        probT = [sb(f"c_probT{i}", [P, NK]) for i in range(2)]
        oss, omean, olog, orstd = (sb(f"c_o{n}", [P, CH]) for n in ("ss", "mean", "log", "rstd"))
        sq = sb("c_sq", [P, P])
        psS = [ps(f"c_psS{m}", 1024) for m in range(2)]
        psT = ps("c_psT", 1024)
        psO = [ps(f"c_psO{i}", 512) for i in range(2)]
        const_in, dve_done, act_step = sem("const_in"), sem("dve_done"), sem("act_step")
        lsum_ready, lexp_ready = sem("lsum_ready"), sem("lexp_ready")
        s_mm, top_ready, exp_done, dif_ready = sem("s_mm"), sem("top_ready"), sem("exp_done"), sem("dif_ready")
        t_mm, t_copied, o_mm, o_ready = sem("t_mm"), sem("t_copied"), sem("o_mm"), sem("o_ready")
        omean_ready, orstd_ready = sem("omean_ready"), sem("orstd_ready")
        block = ctx.enter_context(nc.Block())
        O = s.ho[:].rearrange("p (t n) -> p t n", t=NT)
        HALF = NK // 2

        @block.sync
        def _(sp):
            sp.dma_start(ident[:], a["k_ident"]).then_inc(const_in, 16)
            sp.dma_start(lamp[:], a["c_lambda"][0].partition_broadcast(P)).then_inc(const_in, 16)
            sp.dma_start(subg[:], a["c_subln_g"][0].partition_broadcast(P)).then_inc(const_in, 16)
            prefetch_out(nc, s, a, 1, sp)

        @block.tensor
        def _(pe):
            pe.wait_ge(const_in, 48)

            def scores(u):
                t, h = units[u]
                for m in range(2):
                    if u >= 1:
                        pe.wait_ge(exp_done, 2 * (u - 1) + m + 1)
                    for lo, hi in ((0, 512), (512, NK)):
                        mm = nc.tensor.matmul(psS[m][:, lo:hi], qt[m * HD:(m + 1) * HD, h, t * P:(t + 1) * P],
                                              kt[m * HD:(m + 1) * HD, h, lo:hi], start=True, stop=True)
                    mm.then_inc(s_mm, 1)

            def turn(u):
                pe.wait_ge(dif_ready, u + 1)
                if u >= 1:
                    pe.wait_ge(t_copied, 2 * u)
                for i in range(NT):
                    at = bank_place(i, NT)
                    tr = nc.tensor.transpose(psT[:, at:at + P], dif[:, i * P:(i + 1) * P], ident[:])
                tr.then_inc(t_mm, 1)

            def values(u):
                t, h = units[u]
                pe.wait_ge(t_copied, 2 * (u + 1))
                if u >= 2:
                    pe.wait_ge(o_ready, u - 1)
                for i in range(NT):
                    mm = nc.tensor.matmul(psO[u % 2][:, 0:P], probT[u % 2][:, i * P:(i + 1) * P], v[:, i, h * P:(h + 1) * P],
                                          start=(i == 0), stop=(i == NT - 1))
                mm.then_inc(o_mm, 1)

            scores(0)
            for u in range(n_units):
                if u + 1 < n_units:
                    scores(u + 1)
                if u >= 1:
                    values(u - 1)
                turn(u)
            values(n_units - 1)

        @block.vector
        def _(dve):
            chain = [0]

            def link(ins):
                chain[0] += 1
                ins.then_inc(dve_done, 1)
                dve.wait_ge(dve_done, chain[0])

            dve.wait_ge(const_in, 48)
            link(nc.vector.tensor_tensor(lprod[:], lamp[:, 0:4:2, :], lamp[:, 1:4:2, :], ALU.mult))
            nc.vector.tensor_reduce(lsum[:], lprod[:], AX.X, ALU.add).then_inc(lsum_ready, 1)
            dve.wait_ge(lexp_ready, 1)
            link(nc.vector.tensor_tensor(ldif[:], lexp[:, 1:2], lexp[:, 0:1], ALU.subtract))
            link(nc.vector.tensor_scalar(nlam[:], ldif[:], -LAM_INIT, None, ALU.add))
            link(nc.vector.tensor_scalar(subg[:], subg[:], 1.0 - LAM_INIT, None, ALU.mult))

            def highest(u):
                for m in range(2):
                    dve.wait_ge(s_mm, 2 * u + m + 1)
                    link(nc.vector.tensor_reduce(top[:, m:m + 1], psS[m][:, 0:NK], AX.X, ALU.max))
                    if u >= 1:
                        dve.wait_ge(exp_done, 2 * (u - 1) + m + 1)
                    nc.vector.tensor_scalar(ntop[:, m:m + 1], top[:, m:m + 1], -SCALE, None, ALU.mult).then_inc(top_ready, 1)

            def mix(u):
                dve.wait_ge(exp_done, 2 * u + 2)
                link(nc.vector.reciprocal(inv[:], total[:]))
                link(nc.vector.tensor_tensor(coef[:], inv[:, 1:2], nlam[:], ALU.mult))
                link(nc.vector.tensor_scalar(prob[1][:], prob[1][:], coef[:, 0:1], None, ALU.mult))
                if u >= 1:
                    dve.wait_ge(t_mm, u)
                nc.vector.scalar_tensor_tensor(dif[:], prob[0][:], inv[:, 0:1], prob[1][:], ALU.mult, ALU.add).then_inc(dif_ready, 1)

            def half_copy(u):
                dve.wait_ge(t_mm, u + 1)
                if u >= 2:
                    dve.wait_ge(o_mm, u - 1)
                nc.vector.tensor_copy(probT[u % 2][:, HALF:NK], psT[:, 512:512 + NK - HALF]).then_inc(t_copied, 1)

            def finish(u):
                t, h = units[u]
                dve.wait_ge(o_mm, u + 1)
                nc.vector.tensor_copy(O[:, t, h * P:(h + 1) * P], psO[u % 2][:, 0:P]).then_inc(o_ready, 1)

            def subnorm(t):
                dve.wait_ge(o_ready, (t + 1) * CH)
                for h in range(CH):
                    cols = O[:, t, h * P:(h + 1) * P]
                    link(nc.vector.tensor_tensor_reduce(out=sq[:], in0=cols, in1=cols, scale=1.0, scalar=0.0, op0=ALU.mult, op1=ALU.add,
                                                        accum_out=oss[:, h:h + 1]))
                nc.vector.tensor_scalar(omean[:], oss[:], 1.0 / P, EPS, ALU.mult, ALU.add).then_inc(omean_ready, 1)
                dve.wait_ge(orstd_ready, t + 1)
                for h in range(CH):
                    cols = O[:, t, h * P:(h + 1) * P]
                    link(nc.vector.scalar_tensor_tensor(cols, cols, orstd[:, h:h + 1], subg[:], ALU.mult, ALU.mult))

            highest(0)
            for u in range(n_units):
                mix(u)
                if u + 1 < n_units:
                    highest(u + 1)
                if u >= 1:
                    finish(u - 1)
                    if u % CH == 0:
                        subnorm(u // CH - 1)
                half_copy(u)
            finish(n_units - 1)
            subnorm(SEQ // P - 1)

        @block.scalar
        def _(act):
            acts = [0]

            def link(ins):
                acts[0] += 1
                ins.then_inc(act_step, 1)
                act.wait_ge(act_step, acts[0])

            act.wait_ge(lsum_ready, 1)
            nc.scalar.activation(lexp[:], lsum[:], ACT.Exp).then_inc(lexp_ready, 1)

            def expo(u):
                for m in range(2):
                    act.wait_ge(top_ready, 2 * u + m + 1)
                    if u >= 1:
                        act.wait_ge(dif_ready, u)
                    nc.scalar.activation(prob[m][:], psS[m][:, 0:NK], ACT.Exp, bias=ntop[:, m:m + 1], scale=SCALE,
                                         accum_out=total[:, m:m + 1]).then_inc(exp_done, 1)

            expo(0)
            for u in range(n_units):
                if u + 1 < n_units:
                    expo(u + 1)
                if u >= 1 and u % CH == 0:
                    t = u // CH - 1
                    act.wait_ge(omean_ready, t + 1)
                    link(nc.scalar.activation(olog[:], omean[:], ACT.Ln))
                    nc.scalar.activation(orstd[:], olog[:], ACT.Exp, scale=-0.5).then_inc(orstd_ready, 1)
                act.wait_ge(t_mm, u + 1)
                if u >= 2:
                    act.wait_ge(o_mm, u - 1)
                nc.scalar.copy(probT[u % 2][:, 0:HALF], psT[:, 0:HALF]).then_inc(t_copied, 1)
            t = SEQ // P - 1
            act.wait_ge(omean_ready, t + 1)
            link(nc.scalar.activation(olog[:], omean[:], ACT.Ln))
            nc.scalar.activation(orstd[:], olog[:], ACT.Exp, scale=-0.5).then_inc(orstd_ready, 1)


def mix_out(nc, s, a, l):
    tiles = list(range(NT)) if l == 0 else list(range(CT, NT))
    with ExitStack() as ctx:
        sb = lambda n, sh, dt=F32: ctx.enter_context(nc.sbuf_tensor(f"{n}_{l}", sh, dt))
        sem = phase_semaphores(nc, ctx, f"mix_out{l}")
        ps = lambda n, w: ctx.enter_context(nc.psum_tensor(f"{n}_{l}", [P, w], F32))
        ident = sb("m_ident", [P, P])
        oT = [sb(f"m_oT{i}", [P, D]) for i in range(2)]
        sq = sb("m_sq", [P, D])
        up = sb("m_up", [P, D])
        ssq, mean, logs, rstd = (sb(f"m_{n}", [P, NT]) for n in ("ssq", "mean", "logs", "rstd"))
        psT = [ps(f"m_psT{i}", 1024) for i in range(2)]
        psY = [ps(f"m_psY{i}", 1024) for i in range(2)]
        const_in, dve_done, act_step = sem("const_in"), sem("dve_done"), sem("act_step")
        t_mm, t_copied, y_mm, mean_ready, rstd_ready, y_used = (sem(n) for n in ("t_mm", "t_copied", "y_mm", "mean_ready", "rstd_ready", "y_used"))
        block = ctx.enter_context(nc.Block())
        O = s.ho[:].rearrange("p (t n) -> p t n", t=NT)
        o0 = 0 if l == 0 else CT

        @block.sync
        def _(sp):
            sp.dma_start(ident[:], a["k_ident"]).then_inc(const_in, 16)

        @block.tensor
        def _(pe):
            pe.wait_ge(const_in, 16)

            def turn(i):
                if i >= 2:
                    pe.wait_ge(t_copied, i - 1)
                for k in range(KD):
                    tr = nc.tensor.transpose(psT[i % 2][:, k * P:(k + 1) * P], column(O[:, tiles[i] - o0, :], k), ident[:])
                tr.then_inc(t_mm, 1)

            turn(0)
            for c in range(2):
                pe.wait_ge(s.wo_in[c], 16 * (l + 1))
            for i in range(len(tiles)):
                if i + 1 < len(tiles):
                    turn(i + 1)
                pe.wait_ge(t_copied, i + 1)
                if i >= 2:
                    pe.wait_ge(y_used, i - 1)
                for c in range(2):
                    for k in range(KD):
                        mm = nc.tensor.matmul(psY[i % 2][:, c * 512:(c + 1) * 512], oT[i % 2][:, k * P:(k + 1) * P],
                                              s.ring[c][:, k * 512:(k + 1) * 512], start=(k == 0), stop=(k == KD - 1))
                mm.then_inc(y_mm, 1)

        @block.scalar
        def _(act):
            acts = [0]

            def link(ins):
                acts[0] += 1
                ins.then_inc(act_step, 1)
                act.wait_ge(act_step, acts[0])

            def copy(i):
                act.wait_ge(t_mm, i + 1)
                if i >= 2:
                    act.wait_ge(y_mm, i - 1)
                nc.scalar.copy(oT[i % 2][:], psT[i % 2][:]).then_inc(t_copied, 1)

            copy(0)
            for i in range(len(tiles)):
                if i + 1 < len(tiles):
                    copy(i + 1)
                act.wait_ge(mean_ready, i + 1)
                link(nc.scalar.activation(logs[:, i:i + 1], mean[:, i:i + 1], ACT.Ln))
                nc.scalar.activation(rstd[:, i:i + 1], logs[:, i:i + 1], ACT.Exp, scale=-0.5).then_inc(rstd_ready, 1)

        @block.vector
        def _(dve):
            chain = [0]

            def link(ins):
                chain[0] += 1
                ins.then_inc(dve_done, 1)
                dve.wait_ge(dve_done, chain[0])

            for i, t in enumerate(tiles):
                cond = 1 if t < CT else 0
                y = psY[i % 2][:]
                dve.wait_ge(y_mm, i + 1)
                link(nc.vector.tensor_copy(sq[:], y))
                link(nc.vector.tensor_tensor_reduce(out=up[:], in0=sq[:], in1=sq[:], scale=1.0, scalar=0.0, op0=ALU.mult, op1=ALU.add,
                                                    accum_out=ssq[:, i:i + 1]))
                nc.vector.tensor_scalar(mean[:, i:i + 1], ssq[:, i:i + 1], 1.0 / D, EPS, ALU.mult, ALU.add).then_inc(mean_ready, 1)
                dve.wait_ge(rstd_ready, i + 1)
                up_ins = nc.vector.scalar_tensor_tensor(up[:], sq[:], rstd[:, i:i + 1], s.bc[:, cond, 2, :], ALU.mult, ALU.mult)
                up_ins.then_inc(y_used, 1)
                dve.wait_ge(y_used, i + 1)
                link(nc.vector.tensor_tensor(s.X[:, t, :], s.X[:, t, :], up[:], ALU.add))


def route(nc, s, a, l, tiles, r):
    n_t = len(tiles)
    T = n_t * P
    with ExitStack() as ctx:
        sb = lambda n, sh, dt=F32: ctx.enter_context(nc.sbuf_tensor(f"{n}_{l}", sh, dt))
        sem = phase_semaphores(nc, ctx, f"route{l}")
        ps = lambda n, w: ctx.enter_context(nc.psum_tensor(f"{n}_{l}", [P, w], F32))
        hrow = [sb(f"r_hrow{i}", [P, D]) for i in range(2)]
        ssq, mean, logs, rstd = (sb(f"r_{n}", [P, NT]) for n in ("ssq", "mean", "logs", "rstd"))
        HT = sb("r_HT", [P, KD, T])
        rw = sb("r_rw", [P, KD, E])
        rb = sb("r_rb", [P, E])
        beforef, uptof, earlier = sb("r_beforef", [P, P]), sb("r_uptof", [P, E]), sb("r_earlier", [P, NG * NG])
        before, upto, ones = sb("r_before", [P, P], BF16), sb("r_upto", [P, E], BF16), sb("r_ones", [P, P], BF16)
        part = sb("r_part", [P, 2])
        ex, dn, sc, sel = (sb(f"r_{n}", [P, n_t, E]) for n in ("ex", "dn", "sc", "sel"))
        best = sb("r_best", [P, n_t * NG, 8])
        gs, gm, pen, rank = (sb(f"r_{n}", [P, n_t * NG]) for n in ("gs", "gm", "pen", "rank"))
        gt, eq = sb("r_gt", [P, n_t, NG, NG]), sb("r_eq", [P, n_t, NG, NG])
        msel, left, mask, wt = (sb(f"r_{n}", [P, n_t, E]) for n in ("msel", "left", "mask", "wt"))
        top8 = sb("r_top8", [P, n_t, 8])
        maskb = sb("r_maskb", [P, n_t, E], BF16)
        wsum, winv = sb("r_wsum", [P, n_t]), sb("r_winv", [P, n_t])
        res1 = sb("r_res1", [P, n_t, E])
        cmpT = sb("r_cmpT", [P, KMAX, P])
        nbT = sb("r_nbT", [P, P], BF16)
        cmp = sb("r_cmp", [P, KMAX, E])
        nb = sb("r_nb", [P, E])
        le, lenb = sb("r_le", [P, E]), sb("r_lenb", [P, E])
        bexp, base, over, kb = (sb(f"r_{n}", [P, 1]) for n in ("bexp", "base", "over", "kb"))
        rows = sb("r_rows", [P, 2])
        g = [sb(f"r_g{i}", [P, F]) for i in range(2)]
        ge, gd = sb("r_ge", [P, F]), sb("r_gd", [P, F])
        gT = [sb(f"r_gT{i}", [P, F]) for i in range(2)]
        ysb = [sb(f"r_y{i}", [P, D]) for i in range(2)]
        psT = ps("r_psT", 1024)
        psZ, psH, psG = ps("r_psZ", 512), ps("r_psH", 512), ps("r_psG", 512)
        psY = ps("r_psY", 1024)
        psN = ps("r_psN", 512)
        (bc_in, const_in, sh_in, dve_done, act_step, mean_ready, rstd_ready, hrow_ready, t_mm, ht_ready, z_mm, ex_ready,
         mask_ready, count_mm, nb_ready, end_mm, rows_ready, rows_mm, zero_ready, ones_ready, h_mm, e_ready, g_ready, gt_mm, gt_ready,
         y_mm, y_ready, tab_ready) = (
            sem(n) for n in ("bc_in", "const_in", "sh_in", "dve_done", "act_step", "mean_ready", "rstd_ready", "hrow_ready", "t_mm",
                             "ht_ready", "z_mm", "ex_ready", "mask_ready", "count_mm", "nb_ready", "end_mm", "rows_ready", "rows_mm",
                             "zero_ready", "ones_ready", "h_mm", "e_ready", "g_ready", "gt_mm", "gt_ready", "y_mm", "y_ready", "tab_ready"))
        h_out = [sem(f"h_out{i}") for i in range(2)]
        y_out = [sem(f"y_out{i}") for i in range(2)]
        zero_out = sem("zero_out")
        block = ctx.enter_context(nc.Block())
        w13 = s.ring[0][:].rearrange("p (k n) -> p k n", k=KD)
        w2 = s.ring[2][:].rearrange("p (u k n) -> p u k n", u=2, k=KF)

        @block.sync
        def _(sp):
            load_modulation(nc, s, sp, l, 1, bc_in)
            for dst, src in ((r.ident[:], a["k_ident"]), (rw[:], steps(a["router_w"][l])), (rb[:], a["router_bias"][l].partition_broadcast(P)),
                             (beforef[:], a["k_before"]), (uptof[:], a["k_upto"]), (earlier[:], a["k_earlier"]), (part[:], a["k_part"]),
                             (r.slots[:], a["k_slots"])):
                sp.dma_start(dst, src).then_inc(const_in, 16)
            sp.dma_start(w13[:, :, 0:F], steps(a["sh_w1"][l])).then_inc(sh_in, 16)
            sp.dma_start(w13[:, :, F:2 * F], steps(a["sh_w3"][l])).then_inc(sh_in, 16)
            sp.dma_start(w2[:, 0, :, :], a["sh_w2"][l].rearrange("(p k) n -> p k n", k=KF)).then_inc(sh_in, 16)
            for i in range(n_t):
                sp.wait_ge(hrow_ready, i + 1)
                sp.dma_start(s.hrows[l][i * P:(i + 1) * P, :], hrow[i % 2][:]).then_inc(h_out[i % 2], 16)
            for i in range(n_t):
                sp.wait_ge(y_ready, i + 1)
                sp.dma_start(s.yrows[l][i * P:(i + 1) * P, :], ysb[i % 2][:]).then_inc(y_out[i % 2], 16)
            for i in range(2):
                sp.wait_ge(h_out[i], 16 * n_t // 2)
                sp.wait_ge(y_out[i], 16 * n_t // 2)

        @block.gpsimd
        def _(pool):
            nc.gpsimd.memset(r.zero[:], 0.0).then_inc(zero_ready, 1)
            pool.wait_ge(zero_ready, 1)
            pool.dma_start(s.hrows[l][T:T + P, :], r.zero[:]).then_inc(zero_out, 16)
            pool.dma_start(s.yrows[l][T:T + P, :], r.zero[:]).then_inc(zero_out, 16)
            pool.wait_ge(zero_out, 32)

        @block.tensor
        def _(pe):
            pe.wait_ge(const_in, 128)
            for i in range(n_t):
                pe.wait_ge(hrow_ready, i + 1)
                if i >= 1:
                    pe.wait_ge(ht_ready, i)
                for k in range(KD):
                    tr = nc.tensor.transpose(psT[:, k * P:(k + 1) * P], column(hrow[i % 2][:], k), r.ident[:])
                tr.then_inc(t_mm, 1)
                pe.wait_ge(ht_ready, i + 1)
                for k in range(KD):
                    mm = nc.tensor.matmul(psZ[:, i * E:(i + 1) * E], HT[:, k, i * P:(i + 1) * P], rw[:, k, :], start=(k == 0), stop=(k == KD - 1))
                mm.then_inc(z_mm, 1)

            def shared(i):
                if i == 0:
                    pe.wait_ge(sh_in, 48)
                if i >= 1:
                    pe.wait_ge(g_ready, i)
                for k in range(KD):
                    mm = nc.tensor.matmul(psH[:], HT[:, k, i * P:(i + 1) * P], w13[:, k, :], start=(k == 0), stop=(k == KD - 1))
                mm.then_inc(h_mm, 1)
                pe.wait_ge(g_ready, i + 1)
                if i >= 1:
                    pe.wait_ge(gt_ready, i)
                for k in range(KF):
                    tr = nc.tensor.transpose(psG[:, k * P:(k + 1) * P], g[i % 2][:].rearrange("a (p k) -> a k p", k=KF)[:, k, :], r.ident[:])
                tr.then_inc(gt_mm, 1)
                pe.wait_ge(gt_ready, i + 1)
                if i >= 1:
                    pe.wait_ge(y_ready, i)
                for c in range(2):
                    for k in range(KF):
                        mm = nc.tensor.matmul(psY[:, c * 512:(c + 1) * 512], gT[i % 2][:, k * P:(k + 1) * P], w2[:, 0, k, c * 512:(c + 1) * 512],
                                              start=(k == 0), stop=(k == KF - 1))
                mm.then_inc(y_mm, 1)

            for i in range(n_t):
                shared(i)

            pe.wait_ge(mask_ready, 1)
            pe.wait_ge(ones_ready, 1)
            for i in range(n_t):
                for j in range(i):
                    nc.tensor.matmul(psZ[:, i * E:(i + 1) * E], ones[:], maskb[:, j, :], start=(j == 0), stop=False)
                nc.tensor.matmul(psZ[:, i * E:(i + 1) * E], before[:], maskb[:, i, :], start=(i == 0), stop=True)
            for i in range(n_t):
                nc.tensor.matmul(psN[0:E, 0:P], maskb[:, i, :], ones[:], start=(i == 0), stop=(i == n_t - 1))
            for i in range(n_t):
                mm = nc.tensor.matmul(psN[:, P:P + E], ones[:], maskb[:, i, :], start=(i == 0), stop=(i == n_t - 1))
            mm.then_inc(count_mm, 1)
            pe.wait_ge(nb_ready, 1)
            nc.tensor.matmul(psN[:, 256:256 + E], nbT[0:E, :], upto[0:E, :], start=True, stop=True).then_inc(end_mm, 1)
            pe.wait_ge(rows_ready, 1)
            for j in range(2):
                tr = nc.tensor.transpose(psG[0:1, j * P:(j + 1) * P], rows[:, j:j + 1], r.ident[:])
            tr.then_inc(rows_mm, 1)

        @block.scalar
        def _(act):
            acts = [0]

            def link(ins):
                acts[0] += 1
                ins.then_inc(act_step, 1)
                act.wait_ge(act_step, acts[0])

            act.wait_ge(mean_ready, 1)
            link(nc.scalar.activation(logs[:, 0:n_t], mean[:, 0:n_t], ACT.Ln))
            nc.scalar.activation(rstd[:, 0:n_t], logs[:, 0:n_t], ACT.Exp, scale=-0.5).then_inc(rstd_ready, 1)
            for i in range(n_t):
                act.wait_ge(t_mm, i + 1)
                nc.scalar.copy(HT[:, :, i * P:(i + 1) * P], psT[:].rearrange("p (k n) -> p k n", k=KD)).then_inc(ht_ready, 1)
            act.wait_ge(z_mm, n_t)
            nc.scalar.activation(ex[:], psZ[:, 0:n_t * E].rearrange("p (t e) -> p t e", e=E), ACT.Exp, scale=-1.0).then_inc(ex_ready, 1)
            for i in range(n_t):
                act.wait_ge(h_mm, i + 1)
                if i >= 1:
                    act.wait_ge(g_ready, i)
                nc.scalar.activation(ge[:], psH[:, 0:F], ACT.Exp, scale=-1.0).then_inc(e_ready, 1)
                act.wait_ge(gt_mm, i + 1)
                if i >= 2:
                    act.wait_ge(y_mm, i - 1)
                nc.scalar.copy(gT[i % 2][:], psG[:, 0:F]).then_inc(gt_ready, 1)
                act.wait_ge(y_mm, i + 1)
                if i >= 2:
                    act.wait_ge(y_out[i % 2], 16 * (i // 2))
                nc.scalar.copy(ysb[i % 2][:], psY[:]).then_inc(y_ready, 1)

        @block.vector
        def _(dve):
            chain = [0]

            def link(ins):
                chain[0] += 1
                ins.then_inc(dve_done, 1)
                dve.wait_ge(dve_done, chain[0])

            for i, t in enumerate(tiles):
                link(nc.vector.tensor_tensor_reduce(out=hrow[0][:], in0=s.X[:, t, :], in1=s.X[:, t, :], scale=1.0, scalar=0.0,
                                                    op0=ALU.mult, op1=ALU.add, accum_out=ssq[:, i:i + 1]))
            nc.vector.tensor_scalar(mean[:, 0:n_t], ssq[:, 0:n_t], 1.0 / D, EPS, ALU.mult, ALU.add).then_inc(mean_ready, 1)
            dve.wait_ge(bc_in, 32)
            dve.wait_ge(rstd_ready, 1)
            for i, t in enumerate(tiles):
                cond = 1 if t < CT else 0
                if i >= 2:
                    dve.wait_ge(t_mm, i - 1)
                    dve.wait_ge(h_out[i % 2], 16 * (i // 2))
                link(nc.vector.scalar_tensor_tensor(hrow[i % 2][:], s.X[:, t, :], rstd[:, i:i + 1], s.bc[:, cond, 1, :], ALU.mult, ALU.mult))
                nc.vector.tensor_tensor(hrow[i % 2][:], hrow[i % 2][:], s.bc[:, cond, 0, :], ALU.add).then_inc(hrow_ready, 1)
            dve.wait_ge(const_in, 128)
            link(nc.vector.tensor_copy(before[:], beforef[:]))
            link(nc.vector.tensor_copy(upto[:], uptof[:]))
            nc.vector.memset(ones[:], 1.0).then_inc(ones_ready, 1)

            def shared_gate(i):
                b = i % 2
                dve.wait_ge(e_ready, i + 1)
                link(nc.vector.tensor_scalar(ge[:], ge[:], 1.0, None, ALU.add))
                link(nc.vector.reciprocal(gd[:], ge[:]))
                link(nc.vector.tensor_tensor(gd[:], gd[:], psH[:, 0:F], ALU.mult))
                if i >= 2:
                    dve.wait_ge(gt_mm, i - 1)
                nc.vector.tensor_tensor(g[b][:], gd[:], psH[:, F:2 * F], ALU.mult).then_inc(g_ready, 1)

            shared_gate(0)
            dve.wait_ge(ex_ready, 1)
            link(nc.vector.tensor_scalar(dn[:], ex[:], 1.0, None, ALU.add))
            link(nc.vector.reciprocal(sc[:], dn[:]))
            link(nc.vector.tensor_tensor(sel[:], sc[:], rb[:].unsqueeze(1).to_broadcast([P, n_t, E]), ALU.add))
            flat = sel[:].rearrange("p t (g e) -> p (t g) e", e=EG)
            for j in range(n_t * NG):
                last = nc.vector.max(best[:, j, :], flat[:, j, :])
                if j % NG == NG - 1:
                    link(last)
                if j == 3 * NG - 1:
                    shared_gate(1)
            link(nc.vector.tensor_tensor(gs[:], best[:, :, 0], best[:, :, 1], ALU.add))
            if n_t > 2:
                shared_gate(2)
            g3 = gs[:].rearrange("p (t g) -> p t g", g=NG)
            theirs = g3.unsqueeze(2).to_broadcast([P, n_t, NG, NG])
            own = g3.unsqueeze(3).to_broadcast([P, n_t, NG, NG])
            link(nc.vector.tensor_tensor(gt[:], theirs, own, ALU.is_gt))
            link(nc.vector.tensor_tensor(eq[:], theirs, own, ALU.is_equal))
            eqf, gtf = eq[:].rearrange("p t i j -> p t (i j)"), gt[:].rearrange("p t i j -> p t (i j)")
            link(nc.vector.tensor_tensor(eqf, eqf, earlier[:].unsqueeze(1).to_broadcast([P, n_t, NG * NG]), ALU.mult))
            link(nc.vector.tensor_tensor(gtf, gtf, eqf, ALU.add))
            link(nc.vector.tensor_reduce(rank[:], gt[:].rearrange("p t i j -> p (t i) j"), AX.X, ALU.add))
            link(nc.vector.tensor_scalar(gm[:], rank[:], float(TOPG), None, ALU.is_lt))
            link(nc.vector.tensor_scalar(pen[:], gm[:], -1.0, -NEG, ALU.add, ALU.mult))
            mflat = msel[:].rearrange("p t (g e) -> p (t g) e", e=EG)
            link(nc.vector.tensor_tensor(mflat, flat, gm[:].unsqueeze(2).to_broadcast([P, n_t * NG, EG]), ALU.mult))
            link(nc.vector.tensor_tensor(mflat, mflat, pen[:].unsqueeze(2).to_broadcast([P, n_t * NG, EG]), ALU.add))
            if n_t > 3:
                shared_gate(3)
            for i in range(n_t):
                link(nc.vector.max(top8[:, i, :], msel[:, i, :]))
                link(nc.vector.match_replace(left[:, i, :], top8[:, i, :], msel[:, i, :], -3e38))
            link(nc.vector.tensor_scalar(mask[:], left[:], -2e38, None, ALU.is_lt))
            nc.vector.tensor_copy(maskb[:], mask[:]).then_inc(mask_ready, 1)
            link(nc.vector.tensor_tensor(wt[:], sc[:], mask[:], ALU.mult))
            link(nc.vector.tensor_reduce(wsum[:], wt[:], AX.X, ALU.add))
            link(nc.vector.reciprocal(winv[:], wsum[:]))
            link(nc.vector.tensor_tensor(wt[:], wt[:], winv[:].unsqueeze(2).to_broadcast([P, n_t, E]), ALU.mult))
            link(nc.vector.tensor_scalar(wt[:], wt[:], ROUTED_SCALE, None, ALU.mult))
            for i in range(4, n_t):
                shared_gate(i)
            link(nc.vector.tensor_copy(r.tab5[:, :, :, 0], wt[:]))
            link(nc.vector.tensor_tensor(res1[:], wt[:], r.tab5[:, :, :, 0], ALU.subtract))
            link(nc.vector.tensor_copy(r.tab5[:, :, :, 1], res1[:]))
            link(nc.vector.tensor_tensor(res1[:], res1[:], r.tab5[:, :, :, 1], ALU.subtract))
            link(nc.vector.tensor_copy(r.tab5[:, :, :, 2], res1[:]))
            for i in range(n_t):
                link(nc.vector.memset(r.tab5[:, i, :, 3], float(i * P)))
            link(nc.vector.tensor_copy(r.tab5[:, :, :, 4], part[:, 1:2].unsqueeze(2).to_broadcast([P, n_t, E])))
            link(nc.vector.tensor_scalar(r.spare[:], part[:, 0:1], float(T + 1), None, ALU.add))
            dve.wait_ge(count_mm, 1)
            pos = psZ[:, 0:n_t * E].rearrange("p (t e) -> p t e", e=E)
            link(nc.vector.scalar_tensor_tensor(res1[:], pos, 1.0, mask[:], ALU.add, ALU.mult))
            link(nc.vector.tensor_scalar(r.posm[:].rearrange("p e t -> p t e"), res1[:], -1.0, None, ALU.add))
            for j in range(KMAX):
                link(nc.vector.tensor_scalar(cmpT[0:E, j, :], psN[0:E, 0:P], float(j * P), None, ALU.is_gt))
                link(nc.vector.tensor_scalar(cmp[:, j, :], psN[:, P:P + E], float(j * P), None, ALU.is_gt))
            with nc.allow_low_precision("counts up to 6 are exact"):
                nc.vector.tensor_reduce(nbT[0:E, :], cmpT[0:E].rearrange("p j n -> p n j"), AX.X, ALU.add).then_inc(nb_ready, 1)
            link(nc.vector.tensor_reduce(nb[:], cmp[:].rearrange("p j n -> p n j"), AX.X, ALU.add))
            dve.wait_ge(end_mm, 1)
            end = psN[:, 256:256 + E]
            link(nc.vector.tensor_scalar(le[:], end, part[:, 0:1], None, ALU.is_le))
            link(nc.vector.tensor_tensor(lenb[:], le[:], nb[:], ALU.mult))
            link(nc.vector.tensor_reduce(bexp[:], le[:], AX.X, ALU.add))
            link(nc.vector.tensor_reduce(base[:], lenb[:], AX.X, ALU.add))
            link(nc.vector.tensor_scalar(over[:], bexp[:], float(E), float(KMAX), ALU.is_ge, ALU.mult))
            link(nc.vector.tensor_tensor(kb[:], part[:, 0:1], base[:], ALU.subtract))
            link(nc.vector.tensor_tensor(kb[:], kb[:], over[:], ALU.add))
            link(nc.vector.tensor_scalar(rows[:, 0:1], bexp[:], float(E - 1), None, ALU.min))
            nc.vector.tensor_scalar(rows[:, 1:2], kb[:], float(KMAX), float(P), ALU.min, ALU.mult).then_inc(rows_ready, 1)
            link(nc.vector.tensor_copy(r.table[0:1, 2 * P:2 * P + 1], end[0:1, E - 1:E]))
            link(nc.vector.tensor_scalar(r.table[0:1, 2 * P + 1:2 * P + 2], r.table[0:1, 2 * P:2 * P + 1], 1, None, ALU.logical_shift_right))
            dve.wait_ge(rows_mm, 1)
            nc.vector.tensor_copy(r.table[0:1, 0:2 * P], psG[0:1, 0:2 * P]).then_inc(tab_ready, 1)
            dve.wait_ge(tab_ready, 1)


def wait_for(eng, sem, value):
    if not isinstance(value, int) or value > 0:
        eng.wait_ge(sem, value)


def experts(nc, s, a, l, n_t, r):
    T = n_t * P
    w1 = a["exp_w1"][l].rearrange("e (p k) n -> e p k n", p=P)
    w3 = a["exp_w3"][l].rearrange("e (p k) n -> e p k n", p=P)
    w2 = a["exp_w2"][l].rearrange("e (p k) n -> e p k n", k=KF)
    with ExitStack() as ctx:
        sb = lambda n, sh, dt=F32: ctx.enter_context(nc.sbuf_tensor(f"{n}_{l}", sh, dt))
        sem = phase_semaphores(nc, ctx, f"experts{l}")
        ps = lambda n, w: ctx.enter_context(nc.psum_tensor(f"{n}_{l}", [P, w], F32))
        xg = [sb(f"e_xg{i}", [P, D]) for i in range(2)]
        xT = [sb(f"e_xT{i}", [P, D]) for i in range(2)]
        sel = [sb(f"e_sel{i}", [P, n_t, P], BF16) for i in range(2)]
        gidx = [sb(f"e_gidx{i}", [P, 1], U32) for i in range(2)]
        gw = [sb(f"e_gw{i}", [P, 1]) for i in range(2)]
        sidx = [sb(f"e_sidx{i}", [P, 1], U32) for i in range(2)]
        sw = [sb(f"e_sw{i}", [P, 1]) for i in range(2)]
        tok, gap = sb("e_tok", [P, 1]), sb("e_gap", [P, 1])
        ge, gd, gs, g = sb("e_ge", [P, F]), sb("e_gd", [P, F]), sb("e_gs", [P, F]), sb("e_g", [P, F])
        gT = [sb(f"e_gT{i}", [P, F]) for i in range(2)]
        ysb = [sb(f"e_y{i}", [P, D]) for i in range(2)]
        psT, psY = ps("e_psT", 1024), ps("e_psY", 1024)
        psH, psG, psI = ps("e_psH", 512), ps("e_psG", 512), ps("e_psI", 512)
        w13_in = [sem(f"w13_in{i}") for i in range(2)]
        w2_in = [sem(f"w2_in{i}") for i in range(2)]
        gathered = [sem(f"gathered{i}") for i in range(2)]
        (sel_ready, idx_mm, idx_step, idx_ready, copied, xt_mm, xt_ready, h_mm, e_ready, g_step, g_ready, gt_mm, gt_ready, y_mm,
         y_ready, added, pool_clear) = (sem(n) for n in (
             "sel_ready", "idx_mm", "idx_step", "idx_ready", "copied", "xt_mm", "xt_ready", "h_mm", "e_ready", "g_step", "g_ready",
             "gt_mm", "gt_ready", "y_mm", "y_ready", "added", "pool_clear"))
        block = ctx.enter_context(nc.Block())
        w13_sb = [s.ring[i][:].rearrange("p (k n) -> p k n", k=KD) for i in range(2)]
        w2_sb = [s.ring[2][:, i * 2048:(i + 1) * 2048].rearrange("p (k n) -> p k n", k=KF) for i in range(2)]
        pairs = lambda eng: eng.value_load(r.table[0:1, 2 * P + 1:2 * P + 2], min_val=2, max_val=(P - 4) // 2)

        def expert_of(eng, b):
            return eng.value_load(r.table[0:1, bass.DynSlice(b, 1)], min_val=0, max_val=E - 1)

        def place_of(eng, b):
            return eng.value_load(r.table[0:1, bass.DynSlice(b + P, 1)], min_val=0, max_val=KMAX * P)

        @block.sync
        def _(sp):
            def load(b, m, par):
                e = expert_of(sp, b)
                wait_for(sp, h_mm, b - 1)
                sp.dma_start(w13_sb[par][:, :, 0:F].unsqueeze(1), w1[bass.DynSlice(e, 1)].rearrange("e p k n -> p e k n")).then_inc(w13_in[par], 16)
                sp.dma_start(w13_sb[par][:, :, F:2 * F].unsqueeze(1), w3[bass.DynSlice(e, 1)].rearrange("e p k n -> p e k n")).then_inc(w13_in[par], 16)
                wait_for(sp, y_mm, b - 1)
                sp.dma_start(w2_sb[par].unsqueeze(1), w2[bass.DynSlice(e, 1)].rearrange("e p k n -> p e k n")).then_inc(w2_in[par], 16)

            load(0, 0, 0)
            def pair(i):
                load(2 * i + 1, i, 1)
                load(2 * i + 2, i + 1, 0)

            pair(0)
            with sp.Fori(1, pairs(sp)) as i:
                pair(i)

        @block.gpsimd
        def _(pool):
            def gather(b, par):
                pool.wait_ge(idx_ready, b + 1)
                wait_for(pool, xt_mm, b - 1)
                pool.sem_inc(pool_clear, 1)
                nc.gpsimd.indirect_dma_start(xg[par][:], None, s.hrows[l], bass.IndirectOffsetOnAxis(ap=gidx[par][:, 0:1], axis=0)
                                             ).then_inc(gathered[par], 16)

            def scatter(b, par):
                pool.wait_ge(copied, b + 1)
                pool.wait_ge(y_ready, 2 * b + 2)
                wait_for(pool, added, 16 * b)
                pool.sem_inc(pool_clear, 1)
                nc.gpsimd.indirect_dma_start(s.yrows[l], bass.IndirectOffsetOnAxis(ap=sidx[par][:, 0:1], axis=0), ysb[par][:], None,
                                             compute_op=ALU.add).then_inc(added, 16)

            n = pairs(pool)
            gather(0, 0)
            gather(1, 1)
            gather(2, 0)
            def pair(i):
                gather(2 * i + 3, 1)
                scatter(2 * i, 0)
                gather(2 * i + 4, 0)
                scatter(2 * i + 1, 1)

            pair(0)
            with pool.Fori(1, n) as i:
                pair(i)
            scatter(2 * n, 0)
            pool.wait_ge(added, 16 * (2 * n + 1))
            pool.wait_ge(gathered[0], 16 * (n + 2))
            pool.wait_ge(gathered[1], 16 * (n + 1))

        @block.tensor
        def _(pe):
            def index(b, par):
                e = expert_of(pe, b)
                pe.wait_ge(sel_ready, b + 1)
                wait_for(pe, idx_ready, b)
                for t in range(n_t):
                    mm = nc.tensor.matmul(psI[:, 0:5], sel[par][:, t, :], r.tab5[:, t, bass.DynSlice(e, 1), :],
                                          start=(t == 0), stop=(t == n_t - 1))
                mm.then_inc(idx_mm, 1)

            def turn(b, m, par):
                pe.wait_ge(gathered[par], 16 * m + 16)
                wait_for(pe, xt_ready, 2 * b)
                for k in range(KD):
                    tr = nc.tensor.transpose(psT[:, k * P:(k + 1) * P], column(xg[par][:], k), r.ident[:])
                tr.then_inc(xt_mm, 1)

            def hidden(b, m, par):
                pe.wait_ge(xt_ready, 2 * b + 2)
                pe.wait_ge(w13_in[par], 32 * m + 32)
                wait_for(pe, g_ready, b)
                for k in range(KD):
                    mm = nc.tensor.matmul(psH[:], xT[par][:, k * P:(k + 1) * P], w13_sb[par][:, k, :], start=(k == 0), stop=(k == KD - 1))
                mm.then_inc(h_mm, 1)

            def turn_gate(b):
                pe.wait_ge(g_ready, b + 1)
                wait_for(pe, gt_ready, b)
                for k in range(KF):
                    tr = nc.tensor.transpose(psG[:, k * P:(k + 1) * P], g[:].rearrange("a (p k) -> a k p", k=KF)[:, k, :], r.ident[:])
                tr.then_inc(gt_mm, 1)

            def down(b, m, par):
                pe.wait_ge(gt_ready, b + 1)
                pe.wait_ge(w2_in[par], 16 * m + 16)
                wait_for(pe, y_ready, 2 * b)
                for c in range(2):
                    for k in range(KF):
                        mm = nc.tensor.matmul(psY[:, c * 512:(c + 1) * 512], gT[par][:, k * P:(k + 1) * P], w2_sb[par][:, k, c * 512:(c + 1) * 512],
                                              start=(k == 0), stop=(k == KF - 1))
                mm.then_inc(y_mm, 1)

            n = pairs(pe)
            index(0, 0)
            index(1, 1)
            turn(0, 0, 0)
            hidden(0, 0, 0)
            index(2, 0)
            turn(1, 0, 1)
            def pair(i):
                hidden(2 * i + 1, i, 1)
                index(2 * i + 3, 1)
                turn_gate(2 * i)
                turn(2 * i + 2, i + 1, 0)
                down(2 * i, i, 0)
                hidden(2 * i + 2, i + 1, 0)
                index(2 * i + 4, 0)
                turn_gate(2 * i + 1)
                turn(2 * i + 3, i + 1, 1)
                down(2 * i + 1, i, 1)

            pair(0)
            with pe.Fori(1, n) as i:
                pair(i)
            turn_gate(2 * n)
            down(2 * n, n, 0)

        @block.scalar
        def _(act):
            def expo(b):
                act.wait_ge(h_mm, b + 1)
                wait_for(act, g_ready, b)
                nc.scalar.activation(ge[:], psH[:, 0:F], ACT.Exp, scale=-1.0).then_inc(e_ready, 1)

            def gate(b, par):
                act.wait_ge(gt_mm, b + 1)
                nc.scalar.copy(gT[par][:], psG[:, 0:F]).then_inc(gt_ready, 1)

            def rows_in(b, par):
                act.wait_ge(xt_mm, b + 1)
                wait_for(act, h_mm, b - 1)
                nc.scalar.copy(xT[par][:, 0:512], psT[:, 0:512]).then_inc(xt_ready, 1)

            def rows_out(b, par):
                act.wait_ge(y_mm, b + 1)
                act.wait_ge(copied, b + 1)
                nc.scalar.activation(ysb[par][:, 0:512], psY[:, 0:512], ACT.Copy, scale=sw[par][:, 0:1]).then_inc(y_ready, 1)

            n = pairs(act)
            rows_in(0, 0)
            expo(0)
            rows_in(1, 1)
            def pair(i):
                gate(2 * i, 0)
                rows_in(2 * i + 2, 0)
                expo(2 * i + 1)
                rows_out(2 * i, 0)
                gate(2 * i + 1, 1)
                rows_in(2 * i + 3, 1)
                expo(2 * i + 2)
                rows_out(2 * i + 1, 1)

            pair(0)
            with act.Fori(1, n) as i:
                pair(i)
            gate(2 * n, 0)
            rows_out(2 * n, 0)

        @block.vector
        def _(dve):
            def choose(b, par):
                e, at = expert_of(dve, b), place_of(dve, b)
                wait_for(dve, idx_mm, b - 1)
                nc.vector.tensor_tensor(sel[par][:], r.slots[:, bass.DynSlice(at, P)].unsqueeze(1).to_broadcast([P, n_t, P]),
                                        r.posm[:, bass.DynSlice(e, 1), :].rearrange("p e t -> p t e").to_broadcast([P, n_t, P]),
                                        ALU.is_equal).then_inc(sel_ready, 1)

            def indices(b, par):
                early = isinstance(b, int) and b < 2
                base = 4 * b + (0 if early else 2 * (b - 2))
                if not early:
                    wait_for(dve, added, 16 * (b - 3))
                    nc.vector.tensor_copy(sidx[par][:], gidx[par][:]).then_inc(idx_step, 1)
                    nc.vector.tensor_copy(sw[par][:], gw[par][:]).then_inc(idx_step, 1)
                    dve.wait_ge(idx_step, base + 2)
                    dve.sem_inc(copied, 1)
                    base = base + 2
                dve.wait_ge(idx_mm, b + 1)
                nc.vector.tensor_reduce(gw[par][:], psI[:, 0:3], AX.X, ALU.add).then_inc(idx_step, 1)
                nc.vector.tensor_reduce(tok[:], psI[:, 3:5], AX.X, ALU.add).then_inc(idx_step, 1)
                dve.wait_ge(idx_step, base + 2)
                nc.vector.tensor_scalar(gap[:], tok[:], 0.0, r.spare[:, 0:1], ALU.is_equal, ALU.mult).then_inc(idx_step, 1)
                dve.wait_ge(idx_step, base + 3)
                nc.vector.scalar_tensor_tensor(gidx[par][:], tok[:], -1.0, gap[:], ALU.add, ALU.add).then_inc(idx_step, 1)
                dve.wait_ge(idx_step, base + 4)
                dve.sem_inc(idx_ready, 1)

            def silu(b):
                dve.wait_ge(e_ready, b + 1)
                nc.vector.tensor_scalar(gd[:], ge[:], 1.0, None, ALU.add).then_inc(g_step, 1)
                dve.wait_ge(g_step, 3 * b + 1)
                nc.vector.reciprocal(gs[:], gd[:]).then_inc(g_step, 1)
                dve.wait_ge(g_step, 3 * b + 2)
                nc.vector.tensor_tensor(gd[:], gs[:], psH[:, 0:F], ALU.mult).then_inc(g_step, 1)
                dve.wait_ge(g_step, 3 * b + 3)
                wait_for(dve, gt_mm, b)
                nc.vector.tensor_tensor(g[:], gd[:], psH[:, F:2 * F], ALU.mult).then_inc(g_ready, 1)

            def rows_in(b, par):
                dve.wait_ge(xt_mm, b + 1)
                wait_for(dve, h_mm, b - 1)
                nc.vector.tensor_copy(xT[par][:, 512:1024], psT[:, 512:1024]).then_inc(xt_ready, 1)

            def rows_out(b, par):
                dve.wait_ge(y_mm, b + 1)
                nc.vector.tensor_scalar(ysb[par][:, 512:1024], psY[:, 512:1024], sw[par][:, 0:1], None, ALU.mult).then_inc(y_ready, 1)

            n = pairs(dve)
            choose(0, 0)
            indices(0, 0)
            choose(1, 1)
            indices(1, 1)
            rows_in(0, 0)
            choose(2, 0)
            indices(2, 0)
            silu(0)
            rows_in(1, 1)
            def pair(i):
                choose(2 * i + 3, 1)
                indices(2 * i + 3, 1)
                rows_in(2 * i + 2, 0)
                silu(2 * i + 1)
                rows_out(2 * i, 0)
                choose(2 * i + 4, 0)
                indices(2 * i + 4, 0)
                rows_in(2 * i + 3, 1)
                silu(2 * i + 2)
                rows_out(2 * i + 1, 1)

            pair(0)
            with dve.Fori(1, n) as i:
                pair(i)
            rows_out(2 * n, 0)


def combine(nc, s, a, l, tiles):
    last = l == DEPTH - 1
    with ExitStack() as ctx:
        sb = lambda n, sh, dt=F32: ctx.enter_context(nc.sbuf_tensor(f"{n}_{l}", sh, dt))
        sem = phase_semaphores(nc, ctx, f"combine{l}")
        Y = sb("f_Y", [P, len(tiles), D])
        up = sb("f_up", [P, D])
        ssq, mean, logs, rstd = (sb(f"f_{n}", [P, NT]) for n in ("ssq", "mean", "logs", "rstd"))
        y_in = [sem(f"y_in{i}") for i in range(len(tiles))]
        dve_done, act_step, mean_ready, rstd_ready, x_ready, out_done = (
            sem(n) for n in ("dve_done", "act_step", "mean_ready", "rstd_ready", "x_ready", "out_done"))
        block = ctx.enter_context(nc.Block())

        @block.sync
        def _(sp):
            for i in range(len(tiles)):
                sp.dma_start(Y[:, i, :], s.yrows[l][i * P:(i + 1) * P, :]).then_inc(y_in[i], 16)
            if last:
                out = a["out"].rearrange("o (t p) d -> (o t) p d", p=P)
                for i in range(len(tiles)):
                    sp.wait_ge(x_ready, i + 1)
                    sp.dma_start(out[i], s.X[:, tiles[i], :]).then_inc(out_done, 16)
                sp.wait_ge(out_done, 16 * len(tiles))

        @block.scalar
        def _(act):
            for i in range(len(tiles)):
                act.wait_ge(mean_ready, i + 1)
                nc.scalar.activation(logs[:, i:i + 1], mean[:, i:i + 1], ACT.Ln).then_inc(act_step, 1)
                act.wait_ge(act_step, i + 1)
                nc.scalar.activation(rstd[:, i:i + 1], logs[:, i:i + 1], ACT.Exp, scale=-0.5).then_inc(rstd_ready, 1)

        @block.vector
        def _(dve):
            chain = [0]

            def link(ins):
                chain[0] += 1
                ins.then_inc(dve_done, 1)
                dve.wait_ge(dve_done, chain[0])

            def square(i):
                dve.wait_ge(y_in[i], 16)
                link(nc.vector.tensor_tensor_reduce(out=up[:], in0=Y[:, i, :], in1=Y[:, i, :], scale=1.0, scalar=0.0, op0=ALU.mult,
                                                    op1=ALU.add, accum_out=ssq[:, i:i + 1]))
                nc.vector.tensor_scalar(mean[:, i:i + 1], ssq[:, i:i + 1], 1.0 / D, EPS, ALU.mult, ALU.add).then_inc(mean_ready, 1)

            square(0)
            for i, t in enumerate(tiles):
                if i + 1 < len(tiles):
                    square(i + 1)
                cond = 1 if t < CT else 0
                dve.wait_ge(rstd_ready, i + 1)
                link(nc.vector.scalar_tensor_tensor(Y[:, i, :], Y[:, i, :], rstd[:, i:i + 1], s.bc[:, cond, 2, :], ALU.mult, ALU.mult))
                nc.vector.tensor_tensor(s.X[:, t, :], s.X[:, t, :], Y[:, i, :], ALU.add).then_inc(x_ready, 1)
                dve.wait_ge(x_ready, i + 1)


def hybrid_backbone(nc, a, stop=None):
    with ExitStack() as top:
        s = Core()
        s.X = top.enter_context(nc.sbuf_tensor("X", [P, NT, D], F32))
        s.bc = top.enter_context(nc.sbuf_tensor("bc", [P, 2, 3, D], F32))
        s.ring = [top.enter_context(nc.sbuf_tensor(f"ring{i}", [P, 4096], F32)) for i in range(RING)]
        s.mod = nc.dram_tensor("mod_rows", [DEPTH, 2, 6, D], F32, kind="Internal").ap()
        s.hrows = [nc.dram_tensor(f"h_rows{l}", [(NTOK if l == 0 else SEQ) + P, D], F32, kind="Internal").ap() for l in range(DEPTH)]
        s.yrows = [nc.dram_tensor(f"y_rows{l}", [(NTOK if l == 0 else SEQ) + P, D], F32, kind="Internal").ap() for l in range(DEPTH)]
        s.x_in = top.enter_context(nc.semaphore("x_in"))
        s.wo_in = [top.enter_context(nc.semaphore(f"wo_in{i}")) for i in range(2)]
        adaln(nc, s, a)
        for l in range(DEPTH):
            with ExitStack() as mixer:
                sb = lambda n, sh: mixer.enter_context(nc.sbuf_tensor(f"{n}_{l}", sh, F32))
                s.ho = sb("ho", [P, NT * D])
                qt = sb("qt", [P, 8, NTOK if l == 0 else SEQ])
                kt = sb("kt", [P, 2 if l == 0 else CH, NTOK])
                v = sb("v", [P, NT, 2 * GROUPS_KV * HD if l == 0 else D])
                project(nc, s, a, l, qt, kt, v)
                (attend_ab if l == 0 else attend_c)(nc, s, a, qt, kt, v)
                mix_out(nc, s, a, l)
            tiles = list(range(NT)) if l == 0 else list(range(CT, NT))
            with ExitStack() as moe:
                sb = lambda n, sh, dt=F32: moe.enter_context(nc.sbuf_tensor(f"{n}_{l}", sh, dt))
                r = Core()
                n_t = len(tiles)
                r.ident = sb("m_id", [P, P])
                r.slots = sb("slots", [P, P * (KMAX + 1)])
                r.tab5 = sb("tab5", [P, n_t, E, 5], BF16)
                r.posm = sb("posm", [P, E, n_t])
                r.spare = sb("spare", [P, 1])
                r.table = sb("table", [1, 2 * P + 2], I32)
                r.zero = sb("zero", [P, D])
                route(nc, s, a, l, tiles, r)
                experts(nc, s, a, l, n_t, r)
            combine(nc, s, a, l, tiles)


_INS = ["x", "c", "ctx", "c_ctx", "ada_w", "ada_b", "norm_g", "ab_w_in", "ab_w_out", "a_q_norm", "a_k_norm", "b_sink", "c_w_in",
        "c_w_out", "c_lambda", "c_subln_g", "router_w", "router_bias", "exp_w1", "exp_w3", "exp_w2", "sh_w1", "sh_w3", "sh_w2"]


def kernel(**inputs):
    import concourse.bacc as bacc
    from concourse.bass_utils import run_bass_kernel_spmd

    nc = bacc.Bacc("TRN2", target_bir_lowering=False, num_devices=1)
    arrays, aps = {}, {}
    for name, value in [(n, inputs[n]) for n in _INS] + list(host_constants().items()):
        v = np.ascontiguousarray(value)
        arrays[f"in_{name}"] = v
        aps[name] = nc.dram_tensor(f"in_{name}", v.shape, mybir.dt.from_np(v.dtype), kind="ExternalInput").ap()
    aps["out"] = nc.dram_tensor("out_0", (1, SEQ, D), F32, kind="ExternalOutput").ap()
    hybrid_backbone(nc, aps)
    result = run_bass_kernel_spmd(nc, [arrays], core_ids=[0])
    return result.results[0]["out_0"]
```

```python
import math
from contextlib import ExitStack

import numpy as np

import concourse.bass as bass
from concourse import mybir

F32 = mybir.dt.float32
F32R = mybir.dt.float32r
BF16 = mybir.dt.bfloat16
I32 = mybir.dt.int32
U32 = mybir.dt.uint32
ALU = mybir.AluOpType
ACT = mybir.ActivationFunctionType
AX = mybir.AxisListType

P = 128
D = 1024
KD = D // P
SEQ, CTX = 512, 256
NTOK = SEQ + CTX
NT, CT = NTOK // P, CTX // P
DEPTH = 2
HD = 64
EPS = 1e-6
GRID_W = 64
THETA = 10000.0
WINDOW = 128
AH, GROUPS_KV = 8, 2
SCALE = HD ** -0.5
CH = 8
E, TOPK, NG, TOPG = 64, 8, 8, 4
EG = E // NG
F = 256
KF = F // P
ROUTED_SCALE = 2.5
RING = 3
LAM_INIT = 0.8 - 0.6 * math.exp(-0.3)
KMAX = NTOK // P
NEG = -1e30


def host_constants():
    p = np.arange(P)
    row = np.arange(SEQ)
    inv = (np.float32(THETA) ** (-np.arange(HD // 4, dtype=np.float32) / np.float32(HD // 4))).astype(np.float32)
    ang = np.concatenate([(row // GRID_W).astype(np.float32)[:, None] * inv,
                          (row % GRID_W).astype(np.float32)[:, None] * inv], axis=-1)
    cos, sin = np.cos(ang).astype(np.float32), np.sin(ang).astype(np.float32)
    cos2 = np.repeat(cos, 2, axis=1)
    sin2 = np.stack([-sin, sin], axis=-1).reshape(SEQ, HD)
    rope = np.stack([cos2, sin2], axis=0).reshape(2, SEQ // P, P, HD).transpose(2, 0, 1, 3)
    ident = np.eye(P, dtype=np.float32)
    q, k = p[:, None], p[None, :]
    band = np.stack([np.where(k >= q, 0, NEG), np.where(k <= q, 0, NEG)], axis=1).astype(np.float32)
    before = (p[:, None] < p[None, :]).astype(np.float32)
    upto = np.zeros((P, E), np.float32)
    upto[:E] = (np.arange(E)[:, None] <= np.arange(E)[None, :])
    i, j = np.arange(NG)[:, None], np.arange(NG)[None, :]
    earlier = np.broadcast_to((j < i).astype(np.float32).reshape(1, NG * NG), (P, NG * NG))
    slots = np.broadcast_to(np.arange(P * (KMAX + 1), dtype=np.float32)[None], (P, P * (KMAX + 1)))
    part = np.stack([p, p + 1], axis=1).astype(np.float32)
    return {"k_rope": np.ascontiguousarray(rope), "k_ident": ident, "k_band": band, "k_before": before,
            "k_upto": upto, "k_earlier": np.ascontiguousarray(earlier), "k_slots": np.ascontiguousarray(slots),
            "k_part": part}


def steps(ap):
    return ap.rearrange("(p k) n -> p k n", p=P)


def column(ap, k):
    return ap.rearrange("a (p k) -> a k p", k=KD)[:, k, :]


def bank_place(i, n):
    half = (n + 1) // 2
    return i * P if i < half else 512 + (i - half) * P


def phase_semaphores(nc, ctx, phase):
    used = []

    def sem(name):
        used.append(nc.alloc_semaphore(name=f"{phase}_{name}"))
        return used[-1]

    def clear():
        nc.clear_and_free_semaphores(used)
        nc.all_engine_barrier()

    ctx.callback(clear)
    return sem


class Core:
    pass


def adaln(nc, s, a):
    chunks = DEPTH * 12
    with ExitStack() as ctx:
        sb = lambda n, sh, dt=F32: ctx.enter_context(nc.sbuf_tensor(n, sh, dt))
        sem = phase_semaphores(nc, ctx, "ada")
        cond = sb("cond", [P, 2, KD])
        cexp = sb("cexp", [P, 2, KD])
        cden = sb("cden", [P, 2, KD])
        crec = sb("crec", [P, 2, KD])
        silu = sb("silu", [P, KD, 2])
        bias = sb("ada_bias", [2, DEPTH * 6 * D])
        gains = sb("ada_gains", [2, DEPTH * 4 * D])
        mrow = sb("mrow", [2, 2, D])
        pm = [ctx.enter_context(nc.psum_tensor(f"ada_ps{i}", [P, 512], F32)) for i in range(2)]
        vec_in, ada_in = sem("vec_in"), [sem(f"ada_in{i}") for i in range(RING)]
        cexp_done, silu_step = sem("cexp_done"), sem("silu_step")
        ada_mm, ada_added, row_step, row_ready = sem("ada_mm"), sem("ada_added"), sem("row_step"), sem("row_ready")
        row_out = [sem(f"row_out{i}") for i in range(2)]
        block = ctx.enter_context(nc.Block())

        @block.sync
        def _(sp):
            sp.dma_start(cond[:, 0, :], a["c"].rearrange("o (p k) -> (o p) k", p=P)).then_inc(vec_in, 16)
            sp.dma_start(cond[:, 1, :], a["c_ctx"].rearrange("(p k) -> p k", p=P)).then_inc(vec_in, 16)
            sp.dma_start(bias[:], a["ada_b"].rearrange("l n -> (l n)").partition_broadcast(2)).then_inc(vec_in, 16)
            sp.dma_start(gains[:], a["norm_g"].rearrange("l v d -> (l v d)").partition_broadcast(2)).then_inc(vec_in, 16)
            for n in range(chunks):
                if n >= RING:
                    sp.wait_ge(ada_mm, n - RING + 1)
                sp.dma_start(s.ring[:, n % RING, :].rearrange("p (k n) -> p k n", k=KD),
                             steps(a["ada_w"][n // 12])[:, :, (n % 12) * 512:(n % 12 + 1) * 512]).then_inc(ada_in[n % RING], 16)

        @block.scalar
        def _(act):
            act.wait_ge(vec_in, 64)
            nc.scalar.activation(cexp[:], cond[:], ACT.Exp, scale=-1.0).then_inc(cexp_done, 1)
            act.dma_start(s.X[:, 0:CT, :], a["ctx"].rearrange("o (t p) d -> p (o t) d", p=P)).then_inc(s.x_in, 16)
            act.dma_start(s.X[:, CT:NT, :], a["x"].rearrange("o (t p) d -> p (o t) d", p=P)).then_inc(s.x_in, 16)
            for v in range(DEPTH * 6):
                act.wait_ge(row_ready, v + 1)
                act.dma_start(s.mod[v // 6, :, v % 6, :], mrow[:, v % 2, :]).then_inc(row_out[v % 2], 16)
            for i in range(2):
                act.wait_ge(row_out[i], 16 * DEPTH * 3)
            act.wait_ge(s.x_in, 32)

        @block.vector
        def _(dve):
            dve.wait_ge(cexp_done, 1)
            nc.vector.tensor_scalar(cden[:], cexp[:], 1.0, None, ALU.add).then_inc(silu_step, 1)
            dve.wait_ge(silu_step, 1)
            nc.vector.reciprocal(crec[:], cden[:]).then_inc(silu_step, 1)
            dve.wait_ge(silu_step, 2)
            nc.vector.tensor_tensor(silu[:].rearrange("p k c -> p c k"), cond[:], crec[:], ALU.mult).then_inc(silu_step, 1)
            changed = 0
            for n in range(chunks):
                v, half = n // 2, n % 2
                l, vec = v // 6, v % 6
                row = mrow[:, v % 2, half * 512:(half + 1) * 512]
                dve.wait_ge(ada_mm, n + 1)
                if half == 0 and v >= 2:
                    dve.wait_ge(row_out[v % 2], 16 * (v // 2))
                add = nc.vector.tensor_tensor(row, pm[n % 2][0:2, :], bias[:, l * 6 * D + vec * D + half * 512:l * 6 * D + vec * D + (half + 1) * 512], ALU.add)
                add.then_inc(ada_added, 1)
                dve.wait_ge(ada_added, n + 1)
                if vec in (1, 2, 4, 5):
                    g = gains[:, (l * 4 + {1: 0, 2: 1, 4: 2, 5: 3}[vec]) * D + half * 512:(l * 4 + {1: 0, 2: 1, 4: 2, 5: 3}[vec]) * D + (half + 1) * 512]
                    one = 1.0 if vec in (1, 4) else 0.0
                    nc.vector.scalar_tensor_tensor(row, row, one, g, ALU.add, ALU.mult).then_inc(row_step, 1)
                    changed += 1
                    dve.wait_ge(row_step, changed)
                if half:
                    dve.sem_inc(row_ready, 1)

        @block.tensor
        def _(pe):
            pe.wait_ge(silu_step, 3)
            for n in range(chunks):
                pe.wait_ge(ada_in[n % RING], 16 * (n // RING + 1))
                if n >= 2:
                    pe.wait_ge(ada_added, n - 1)
                for k in range(KD):
                    mm = nc.tensor.matmul(pm[n % 2][0:2, :], silu[:, k, :], s.ring[:, n % RING, k * 512:(k + 1) * 512],
                                          start=(k == 0), stop=(k == KD - 1))
                mm.then_inc(ada_mm, 1)


def load_modulation(nc, s, eng, l, half, done):
    for cond in range(2):
        eng.dma_start(s.bc[:, cond, :, :], s.mod[l, cond, 3 * half:3 * half + 3, :].partition_broadcast(P)).then_inc(done, 16)


def sections(l):
    if l == 0:
        return [dict(cols=[(0, 512)], tiles=range(NT), kind="q", norm="q", base=0),
                dict(cols=[(768, 1280)], tiles=range(NT), kind="q", norm=None, base=4),
                dict(cols=[(512, 768), (1280, 1536)], tiles=range(NT), kind="kv", norm="k", base=0)]
    return ([dict(cols=[(i * 512, i * 512 + 512)], tiles=range(CT, NT), kind="q", norm=None, base=4 * i) for i in range(2)]
            + [dict(cols=[(D + i * 512, D + i * 512 + 512)], tiles=range(NT), kind="k", norm=None, base=4 * i) for i in range(2)]
            + [dict(cols=[(2 * D + i * 512, 2 * D + i * 512 + 512)], tiles=range(NT), kind="v", norm=None, base=i) for i in range(2)])


def project(nc, s, a, l, qt, kt, v):
    chunks = sections(l)
    items = [(c, t) for c in range(len(chunks)) for t in chunks[c]["tiles"]]
    w_in = steps((a["ab_w_in"] if l == 0 else a["c_w_in"])[0])
    q0 = 0 if l == 0 else CT
    LAG = 2
    with ExitStack() as ctx:
        sb = lambda n, sh, dt=F32: ctx.enter_context(nc.sbuf_tensor(f"{n}_{l}", sh, dt))
        sem = phase_semaphores(nc, ctx, f"project{l}")
        ps = lambda n, w: ctx.enter_context(nc.psum_tensor(f"{n}_{l}", [P, w], F32))
        ident = sb("p_ident", [P, P])
        rope = sb("p_rope", [P, 2, SEQ // P, HD])
        gains = sb("p_gains", [P, 2, HD])
        hrow = [sb(f"hrow{i}", [P, D]) for i in range(2)]
        ssq, mean, logs, rstd = (sb(f"p_{n}", [P, NT]) for n in ("ssq", "mean", "logs", "rstd"))
        proj = [sb(f"proj{i}", [P, 512]) for i in range(2)]
        rot = [sb(f"rot{i}", [P, 512]) for i in range(2)]
        norm = sb("p_norm", [P, 512])
        t1 = sb("p_t1", [P, 512])
        hss, hmean, hlog, hrstd = (sb(f"ph_{n}", [P, 8]) for n in ("ss", "mean", "log", "rstd"))
        psT = [ps(f"psT{i}", 1024) for i in range(2)]
        psP = [ps(f"psP{i}", 512) for i in range(2)]
        psQ = [ps(f"psQ{i}", 512) for i in range(2)]
        w_at = [sem(f"w_in{i}") for i in range(RING)]
        const_in, bc_in = sem("const_in"), sem("bc_in")
        dve_done, mean_ready, rstd_ready = sem("dve_done"), sem("mean_ready"), sem("rstd_ready")
        hrow_ready, t_mm, ht_ready = sem("hrow_ready"), sem("t_mm"), sem("ht_ready")
        p_mm, p_copied, proj_read = sem("p_mm"), sem("p_copied"), sem("proj_read")
        hmean_ready, hrstd_ready = sem("hmean_ready"), sem("hrstd_ready")
        rot_ready, q_mm, q_copied, act_step = sem("rot_ready"), sem("q_mm"), sem("q_copied"), sem("act_step")
        block = ctx.enter_context(nc.Block())
        HT = s.ho[:].rearrange("p (k n) -> p k n", k=KD)
        normed = [i for i, (c, t) in enumerate(items) if chunks[c]["norm"]]

        @block.sync
        def _(sp):
            load_modulation(nc, s, sp, l, 0, bc_in)
            sp.dma_start(ident[:], a["k_ident"]).then_inc(const_in, 16)
            sp.dma_start(rope[:], a["k_rope"]).then_inc(const_in, 16)
            sp.dma_start(gains[:, 0, :], a["a_q_norm"][0].partition_broadcast(P)).then_inc(const_in, 16)
            sp.dma_start(gains[:, 1, :], a["a_k_norm"][0].partition_broadcast(P)).then_inc(const_in, 16)
            for c, ch in enumerate(chunks):
                if c >= RING:
                    sp.wait_ge(p_mm, sum(len(x["tiles"]) for x in chunks[:c - RING + 1]))
                dst = s.ring[:, c % RING, :].rearrange("p (k n) -> p k n", k=KD)
                at = 0
                for lo, hi in ch["cols"]:
                    sp.dma_start(dst[:, :, at:at + hi - lo], w_in[:, :, lo:hi]).then_inc(w_at[c % RING], 16)
                    at += hi - lo

        def w_need(c):
            return 16 * sum(len(chunks[i]["cols"]) for i in range(c % RING, c + 1, RING))

        @block.vector
        def _(dve):
            chain = [0]

            def link(ins):
                chain[0] += 1
                ins.then_inc(dve_done, 1)
                dve.wait_ge(dve_done, chain[0])

            for t in range(NT):
                link(nc.vector.tensor_tensor_reduce(out=hrow[0][:], in0=s.X[:, t, :], in1=s.X[:, t, :], scale=1.0, scalar=0.0,
                                                    op0=ALU.mult, op1=ALU.add, accum_out=ssq[:, t:t + 1]))
            nc.vector.tensor_scalar(mean[:], ssq[:], 1.0 / D, EPS, ALU.mult, ALU.add).then_inc(mean_ready, 1)
            dve.wait_ge(bc_in, 32)
            dve.wait_ge(rstd_ready, 1)
            for t in range(NT):
                cond = 1 if t < CT else 0
                if t >= 2:
                    dve.wait_ge(t_mm, t - 1)
                link(nc.vector.scalar_tensor_tensor(hrow[t % 2][:], s.X[:, t, :], rstd[:, t:t + 1], s.bc[:, cond, 1, :], ALU.mult, ALU.mult))
                nc.vector.tensor_tensor(hrow[t % 2][:], hrow[t % 2][:], s.bc[:, cond, 0, :], ALU.add).then_inc(hrow_ready, 1)
            dve.wait_ge(const_in, 64)

            def bcast(ap, n):
                return ap.unsqueeze(1).to_broadcast([P, n, HD])

            def head_part(n, t, src, dst, heads, gain):
                flat = src
                if gain is not None:
                    sq = t1[:, 0:heads * HD].rearrange("p (h d) -> p h d", d=HD)
                    link(nc.vector.tensor_tensor(sq, flat, flat, ALU.mult))
                    link(nc.vector.tensor_reduce(hss[:, 0:heads], sq, AX.X, ALU.add))
                    nc.vector.tensor_scalar(hmean[:, 0:heads], hss[:, 0:heads], 1.0 / HD, EPS, ALU.mult, ALU.add).then_inc(hmean_ready, 1)
                    dve.wait_ge(hrstd_ready, normed.index(n) + 1)
                    nv = norm[:, 0:heads * HD].rearrange("p (h d) -> p h d", d=HD)
                    link(nc.vector.tensor_tensor(nv, flat, hrstd[:, 0:heads].unsqueeze(2).to_broadcast([P, heads, HD]), ALU.mult))
                    if t < CT:
                        link(nc.vector.tensor_tensor(dst, regroup(nv, heads), gain4(gain, heads), ALU.mult))
                        return
                    link(nc.vector.tensor_tensor(nv, nv, bcast(gains[:, gain, :], heads), ALU.mult))
                    flat = nv
                elif t < CT:
                    link(nc.vector.tensor_copy(dst, regroup(flat, heads)))
                    return
                cos, sin = rope[:, 0, t - CT, :], rope[:, 1, t - CT, :]
                tv = t1[:, 0:heads * HD].rearrange("p (h d) -> p h d", d=HD)
                tp = tv.rearrange("p h (i e) -> p h i e", e=2)
                fp = flat.rearrange("p h (i e) -> p h i e", e=2)
                sp2 = sin.rearrange("p (i e) -> p i e", e=2)
                for e in range(2):
                    link(nc.vector.tensor_tensor(tp[:, :, :, e], fp[:, :, :, 1 - e],
                                                 sp2[:, :, e].unsqueeze(1).to_broadcast([P, heads, HD // 2]), ALU.mult))
                if flat is src:
                    nv = norm[:, 0:heads * HD].rearrange("p (h d) -> p h d", d=HD)
                link(nc.vector.tensor_tensor(nv, flat, bcast(cos, heads), ALU.mult))
                link(nc.vector.tensor_tensor(dst, regroup(nv, heads), regroup(tv, heads), ALU.add))

            def split(heads):
                return l == 0 and heads == AH

            def regroup(ap, heads):
                return ap.rearrange("p (g j) d -> p g j d", g=GROUPS_KV) if split(heads) else ap

            def gain4(gain, heads):
                g = gains[:, gain, :]
                if split(heads):
                    return g.unsqueeze(1).unsqueeze(1).to_broadcast([P, GROUPS_KV, heads // GROUPS_KV, HD])
                return bcast(g, heads)

            for n, (c, t) in enumerate(items):
                ch = chunks[c]
                if ch["kind"] == "v":
                    continue
                dve.wait_ge(p_copied, n + 1)
                if n >= LAG:
                    dve.wait_ge(q_mm, n - LAG + 1)
                pr = proj[n % 2][:].rearrange("p (h d) -> p h d", d=HD)
                if ch["kind"] == "kv":
                    rt = rot[n % 2][:].rearrange("p (h d) -> p h d", d=HD)
                    head_part(n, t, pr[:, 0:2, :], rt[:, 0:2, :], 2, 1)
                    head_part(n, t, pr[:, 4:6, :], rt[:, 2:4, :], 2, None)
                elif l == 0:
                    head_part(n, t, pr, rot[n % 2][:].rearrange("p (j g d) -> p g j d", g=GROUPS_KV, d=HD), AH, 0 if ch["norm"] else None)
                else:
                    head_part(n, t, pr, rot[n % 2][:].rearrange("p (h d) -> p h d", d=HD), 8, None)
                dve.sem_inc(rot_ready, 1)

        @block.scalar
        def _(act):
            acts = [0]

            def link(ins):
                acts[0] += 1
                ins.then_inc(act_step, 1)
                act.wait_ge(act_step, acts[0])

            act.wait_ge(mean_ready, 1)
            link(nc.scalar.activation(logs[:], mean[:], ACT.Ln))
            nc.scalar.activation(rstd[:], logs[:], ACT.Exp, scale=-0.5).then_inc(rstd_ready, 1)
            for t in range(NT):
                act.wait_ge(t_mm, t + 1)
                nc.scalar.copy(HT[:, :, t * P:(t + 1) * P], psT[t % 2][:].rearrange("p (k n) -> p k n", k=KD)).then_inc(ht_ready, 1)

            def move_out(n):
                c, t = items[n]
                ch = chunks[c]
                if ch["kind"] == "v":
                    return
                act.wait_ge(q_mm, n + 1)
                if ch["kind"] == "kv":
                    out, src = kt[:, 0:2, t * P:(t + 1) * P], psQ[n % 2][:, 0:256]
                elif ch["kind"] == "k":
                    out, src = kt[:, ch["base"]:ch["base"] + 4, t * P:(t + 1) * P], psQ[n % 2][:]
                else:
                    out, src = qt[:, ch["base"]:ch["base"] + 4, (t - q0) * P:(t - q0 + 1) * P], psQ[n % 2][:]
                nc.scalar.copy(out, src.rearrange("p (j n) -> p j n", n=P)).then_inc(q_copied, 1)

            for n, (c, t) in enumerate(items):
                ch = chunks[c]
                act.wait_ge(p_mm, n + 1)
                if ch["kind"] == "v":
                    nc.scalar.copy(v[:, t, ch["base"] * 512:ch["base"] * 512 + 512], psP[n % 2][:]).then_inc(p_copied, 1)
                else:
                    if n >= 2:
                        act.wait_ge(rot_ready, n - 1)
                    if ch["kind"] == "kv":
                        link(nc.scalar.copy(v[:, t, :].rearrange("p (u n) -> p u n", u=2),
                                            psP[n % 2][:].rearrange("p (u w n) -> p u w n", u=2, w=2)[:, :, 1, :]))
                    nc.scalar.copy(proj[n % 2][:], psP[n % 2][:]).then_inc(p_copied, 1)
                if n in normed:
                    h = AH if ch["kind"] == "q" else GROUPS_KV
                    act.wait_ge(hmean_ready, normed.index(n) + 1)
                    link(nc.scalar.activation(hlog[:, 0:h], hmean[:, 0:h], ACT.Ln))
                    nc.scalar.activation(hrstd[:, 0:h], hlog[:, 0:h], ACT.Exp, scale=-0.5).then_inc(hrstd_ready, 1)
                if n >= LAG:
                    move_out(n - LAG)
            for n in range(len(items) - LAG, len(items)):
                move_out(n)

        @block.tensor
        def _(pe):
            pe.wait_ge(const_in, 64)
            for t in range(NT):
                pe.wait_ge(hrow_ready, t + 1)
                if t >= 2:
                    pe.wait_ge(ht_ready, t - 1)
                for k in range(KD):
                    tr = nc.tensor.transpose(psT[t % 2][:, k * P:(k + 1) * P], column(hrow[t % 2][:], k), ident[:])
                tr.then_inc(t_mm, 1)

            def turn(n):
                c, t = items[n]
                kind = chunks[c]["kind"]
                if kind == "v":
                    return
                pe.wait_ge(rot_ready, n + 1)
                if n >= 2:
                    pe.wait_ge(q_copied, n - 1)
                for j in range(2 if kind == "kv" else 4):
                    tr = nc.tensor.transpose(psQ[n % 2][:, j * P:(j + 1) * P], rot[n % 2][:, j * P:(j + 1) * P], ident[:])
                tr.then_inc(q_mm, 1)

            for n, (c, t) in enumerate(items):
                pe.wait_ge(w_at[c % RING], w_need(c))
                pe.wait_ge(ht_ready, min(t + 1, NT))
                if n >= 2:
                    pe.wait_ge(p_copied, n - 1)
                for k in range(KD):
                    mm = nc.tensor.matmul(psP[n % 2][:], HT[:, k, t * P:(t + 1) * P], s.ring[:, c % RING, k * 512:(k + 1) * 512],
                                          start=(k == 0), stop=(k == KD - 1))
                mm.then_inc(p_mm, 1)
                if n >= LAG:
                    turn(n - LAG)
            for n in range(len(items) - LAG, len(items)):
                turn(n)


def prefetch_out(nc, s, a, l, sp):
    w_out = steps((a["ab_w_out"] if l == 0 else a["c_w_out"])[0])
    for c in range(2):
        sp.dma_start(s.ring[:, c, :].rearrange("p (k n) -> p k n", k=KD), w_out[:, :, c * 512:(c + 1) * 512]).then_inc(s.wo_in[c], 16)


def attend_ab(nc, s, a, qt, kt, v):
    units = []
    for t in range(NT):
        for kind in range(2):
            if t < CT:
                keys = [(i, None) for i in range(CT)]
            elif kind == 0:
                keys = [(i, None) for i in range(NT)]
            else:
                near = [i for i in (t - 1, t, t + 1) if CT <= i < NT]
                keys = [(i, None) for i in range(CT)] + [(i, {-1: 0, 0: None, 1: 1}[i - t]) for i in near]
            for h in range(AH):
                units.append((t, kind, h, keys))

    def pieces(keys):
        out = []
        for i, (k, _) in enumerate(keys):
            if out and out[-1][1] + out[-1][2] == k and i % 4:
                out[-1][2] += 1
            else:
                out.append([i, k, 1])
        return out

    n_units = len(units)
    with ExitStack() as ctx:
        sb = lambda n, sh, dt=F32: ctx.enter_context(nc.sbuf_tensor(n, sh, dt))
        sem = phase_semaphores(nc, ctx, "attend_ab")
        ps = lambda n, w: ctx.enter_context(nc.psum_tensor(n, [P, w], F32))
        ident = sb("a_ident", [P, P])
        band = sb("a_band", [P, 2, P])
        sink = sb("a_sink", [P, AH])
        nsink = sb("a_nsink", [P, AH])
        top = sb("a_top", [P, 2])
        ntop = sb("a_ntop", [P, 2])
        total = sb("a_total", [P, 4])
        esink = sb("a_esink", [P, 4])
        den = sb("a_den", [P, 4])
        inv = sb("a_inv", [P, 4])
        prob = [sb(f"a_prob{i}", [P, NT * P]) for i in range(2)]
        probT = [sb(f"a_probT{i}", [P, NT * P]) for i in range(2)]
        psS = [ps(f"a_psS{i}", 1024) for i in range(2)]
        psT = ps("a_psT", 1024)
        psO = [ps(f"a_psO{i}", 512) for i in range(2)]
        const_in, dve_done = sem("const_in"), sem("dve_done")
        s_mm, top_ready, exp_done = sem("s_mm"), sem("top_ready"), sem("exp_done")
        t_mm, t_copied, o_mm, o_ready, den_ready = sem("t_mm"), sem("t_copied"), sem("o_mm"), sem("o_ready"), sem("den_ready")
        block = ctx.enter_context(nc.Block())
        O = s.ho[:].rearrange("p (t n) -> p t n", t=NT)

        @block.sync
        def _(sp):
            sp.dma_start(ident[:], a["k_ident"]).then_inc(const_in, 16)
            sp.dma_start(band[:], a["k_band"]).then_inc(const_in, 16)
            sp.dma_start(sink[:], a["b_sink"][0].partition_broadcast(P)).then_inc(const_in, 16)
            prefetch_out(nc, s, a, 0, sp)

        @block.tensor
        def _(pe):
            pe.wait_ge(const_in, 48)

            def scores(u):
                t, kind, h, keys = units[u]
                g, j = h // 4, h % 4
                if u >= 2:
                    pe.wait_ge(exp_done, u - 1)
                for at, k0, n in pieces(keys):
                    mm = nc.tensor.matmul(psS[u % 2][:, at * P:(at + n) * P], qt[g * HD:(g + 1) * HD, kind * 4 + j, t * P:(t + 1) * P],
                                          kt[g * HD:(g + 1) * HD, kind, k0 * P:(k0 + n) * P], start=True, stop=True)
                mm.then_inc(s_mm, 1)

            def turn(u):
                pe.wait_ge(exp_done, u + 1)
                if u >= 1:
                    pe.wait_ge(t_copied, 2 * u)
                nk = len(units[u][3])
                for i in range(nk):
                    at = bank_place(i, nk)
                    tr = nc.tensor.transpose(psT[:, at:at + P], prob[u % 2][:, i * P:(i + 1) * P], ident[:])
                tr.then_inc(t_mm, 1)

            def values(u):
                t, kind, h, keys = units[u]
                g = h // 4
                pe.wait_ge(t_copied, 2 * (u + 1))
                if u >= 2:
                    pe.wait_ge(o_ready, u - 1)
                for i, (k, _) in enumerate(keys):
                    mm = nc.tensor.matmul(psO[u % 2][:, 0:HD], probT[u % 2][:, i * P:(i + 1) * P],
                                          v[:, k, kind * P + g * HD:kind * P + (g + 1) * HD], start=(i == 0), stop=(i == len(keys) - 1))
                mm.then_inc(o_mm, 1)

            scores(0)
            for u in range(n_units):
                if u + 1 < n_units:
                    scores(u + 1)
                if u >= 1:
                    values(u - 1)
                turn(u)
            values(n_units - 1)

        @block.vector
        def _(dve):
            chain = [0]

            def link(ins):
                chain[0] += 1
                ins.then_inc(dve_done, 1)
                dve.wait_ge(dve_done, chain[0])

            dve.wait_ge(const_in, 48)
            link(nc.vector.tensor_scalar(nsink[:], sink[:], -1.0, None, ALU.mult))

            def highest(u):
                t, kind, h, keys = units[u]
                dve.wait_ge(s_mm, u + 1)
                for i, (_, edge) in enumerate(keys):
                    if edge is not None:
                        cols = psS[u % 2][:, i * P:(i + 1) * P]
                        link(nc.vector.tensor_tensor(cols, cols, band[:, edge, :], ALU.add))
                b = u % 2
                if u >= 2:
                    dve.wait_ge(den_ready, u - 1)
                link(nc.vector.tensor_reduce(top[:, b:b + 1], psS[b][:, 0:len(keys) * P], AX.X, ALU.max))
                if kind == 1:
                    link(nc.vector.tensor_scalar(ntop[:, b:b + 1], top[:, b:b + 1], -SCALE, nsink[:, h:h + 1], ALU.mult, ALU.min))
                else:
                    link(nc.vector.tensor_scalar(ntop[:, b:b + 1], top[:, b:b + 1], -SCALE, None, ALU.mult))
                dve.sem_inc(top_ready, 1)

            def half_copy(u):
                nk = len(units[u][3])
                n, cut = nk * P, (nk + 1) // 2 * P
                dve.wait_ge(t_mm, u + 1)
                if u >= 2:
                    dve.wait_ge(o_mm, u - 1)
                nc.vector.tensor_copy(probT[u % 2][:, cut:n], psT[:, 512:512 + n - cut]).then_inc(t_copied, 1)

            def finish(u):
                t, kind, h, keys = units[u]
                b = u % 4
                dve.wait_ge(den_ready, u + 1)
                if kind == 1:
                    link(nc.vector.tensor_tensor(den[:, b:b + 1], total[:, b:b + 1], esink[:, b:b + 1], ALU.add))
                    link(nc.vector.reciprocal(inv[:, b:b + 1], den[:, b:b + 1]))
                else:
                    link(nc.vector.reciprocal(inv[:, b:b + 1], total[:, b:b + 1]))
                dve.wait_ge(o_mm, u + 1)
                nc.vector.tensor_scalar(O[:, t, kind * 512 + h * HD:kind * 512 + (h + 1) * HD], psO[u % 2][:, 0:HD],
                                        inv[:, b:b + 1], None, ALU.mult).then_inc(o_ready, 1)

            highest(0)
            for u in range(n_units):
                if u + 1 < n_units:
                    highest(u + 1)
                if u >= 1:
                    finish(u - 1)
                half_copy(u)
            finish(n_units - 1)

        @block.scalar
        def _(act):
            for u in range(n_units):
                t, kind, h, keys = units[u]
                n = len(keys) * P
                b = u % 4
                act.wait_ge(top_ready, u + 1)
                if u >= 2:
                    act.wait_ge(t_mm, u - 1)
                if u >= 4:
                    act.wait_ge(o_ready, u - 3)
                nc.scalar.activation(prob[u % 2][:, 0:n], psS[u % 2][:, 0:n], ACT.Exp, bias=ntop[:, u % 2:u % 2 + 1], scale=SCALE,
                                     accum_out=total[:, b:b + 1]).then_inc(exp_done, 1)
                if kind == 1:
                    nc.scalar.activation(esink[:, b:b + 1], sink[:, h:h + 1], ACT.Exp, bias=ntop[:, u % 2:u % 2 + 1]).then_inc(den_ready, 1)
                else:
                    act.wait_ge(exp_done, u + 1)
                    act.sem_inc(den_ready, 1)
                cut = (len(keys) + 1) // 2 * P
                act.wait_ge(t_mm, u + 1)
                if u >= 2:
                    act.wait_ge(o_mm, u - 1)
                nc.scalar.copy(probT[u % 2][:, 0:cut], psT[:, 0:cut]).then_inc(t_copied, 1)


def attend_c(nc, s, a, qt, kt, v):
    units = [(t, h) for t in range(SEQ // P) for h in range(CH)]
    n_units = len(units)
    NK = NT * P
    with ExitStack() as ctx:
        sb = lambda n, sh, dt=F32: ctx.enter_context(nc.sbuf_tensor(n, sh, dt))
        sem = phase_semaphores(nc, ctx, "attend_c")
        ps = lambda n, w: ctx.enter_context(nc.psum_tensor(n, [P, w], F32))
        ident = sb("c_ident", [P, P])
        lamp = sb("c_lamp", [P, 4, HD])
        lprod = sb("c_lprod", [P, 2, HD])
        lsum, lexp = sb("c_lsum", [P, 2]), sb("c_lexp", [P, 2])
        ldif, nlam = sb("c_ldif", [P, 1]), sb("c_nlam", [P, 1])
        subg = sb("c_subg", [P, P])
        top, ntop = sb("c_top", [P, 2]), sb("c_ntop", [P, 2])
        total, inv, coef = sb("c_total", [P, 2]), sb("c_inv", [P, 2]), sb("c_coef", [P, 1])
        prob = [sb(f"c_prob{m}", [P, NK]) for m in range(2)]
        dif = sb("c_dif", [P, NK])
        probT = [sb(f"c_probT{i}", [P, NK]) for i in range(2)]
        oss, omean, olog, orstd = (sb(f"c_o{n}", [P, CH]) for n in ("ss", "mean", "log", "rstd"))
        sq = sb("c_sq", [P, P])
        psS = [ps(f"c_psS{m}", 1024) for m in range(2)]
        psT = ps("c_psT", 1024)
        psO = [ps(f"c_psO{i}", 512) for i in range(2)]
        const_in, dve_done, act_step = sem("const_in"), sem("dve_done"), sem("act_step")
        lsum_ready, lexp_ready = sem("lsum_ready"), sem("lexp_ready")
        s_mm, top_ready, exp_done, dif_ready = sem("s_mm"), sem("top_ready"), sem("exp_done"), sem("dif_ready")
        t_mm, t_copied, o_mm, o_ready = sem("t_mm"), sem("t_copied"), sem("o_mm"), sem("o_ready")
        omean_ready, orstd_ready = sem("omean_ready"), sem("orstd_ready")
        block = ctx.enter_context(nc.Block())
        O = s.ho[:].rearrange("p (t n) -> p t n", t=NT)
        HALF = NK // 2

        @block.sync
        def _(sp):
            sp.dma_start(ident[:], a["k_ident"]).then_inc(const_in, 16)
            sp.dma_start(lamp[:], a["c_lambda"][0].partition_broadcast(P)).then_inc(const_in, 16)
            sp.dma_start(subg[:], a["c_subln_g"][0].partition_broadcast(P)).then_inc(const_in, 16)
            prefetch_out(nc, s, a, 1, sp)

        @block.tensor
        def _(pe):
            pe.wait_ge(const_in, 48)

            def scores(u):
                t, h = units[u]
                for m in range(2):
                    if u >= 1:
                        pe.wait_ge(exp_done, 2 * (u - 1) + m + 1)
                    for lo, hi in ((0, 512), (512, NK)):
                        mm = nc.tensor.matmul(psS[m][:, lo:hi], qt[m * HD:(m + 1) * HD, h, t * P:(t + 1) * P],
                                              kt[m * HD:(m + 1) * HD, h, lo:hi], start=True, stop=True)
                    mm.then_inc(s_mm, 1)

            def turn(u):
                pe.wait_ge(dif_ready, u + 1)
                if u >= 1:
                    pe.wait_ge(t_copied, 2 * u)
                for i in range(NT):
                    at = bank_place(i, NT)
                    tr = nc.tensor.transpose(psT[:, at:at + P], dif[:, i * P:(i + 1) * P], ident[:])
                tr.then_inc(t_mm, 1)

            def values(u):
                t, h = units[u]
                pe.wait_ge(t_copied, 2 * (u + 1))
                if u >= 2:
                    pe.wait_ge(o_ready, u - 1)
                for i in range(NT):
                    mm = nc.tensor.matmul(psO[u % 2][:, 0:P], probT[u % 2][:, i * P:(i + 1) * P], v[:, i, h * P:(h + 1) * P],
                                          start=(i == 0), stop=(i == NT - 1))
                mm.then_inc(o_mm, 1)

            scores(0)
            for u in range(n_units):
                if u + 1 < n_units:
                    scores(u + 1)
                if u >= 1:
                    values(u - 1)
                turn(u)
            values(n_units - 1)

        @block.vector
        def _(dve):
            chain = [0]

            def link(ins):
                chain[0] += 1
                ins.then_inc(dve_done, 1)
                dve.wait_ge(dve_done, chain[0])

            dve.wait_ge(const_in, 48)
            link(nc.vector.tensor_tensor(lprod[:], lamp[:, 0:4:2, :], lamp[:, 1:4:2, :], ALU.mult))
            nc.vector.tensor_reduce(lsum[:], lprod[:], AX.X, ALU.add).then_inc(lsum_ready, 1)
            dve.wait_ge(lexp_ready, 1)
            link(nc.vector.tensor_tensor(ldif[:], lexp[:, 1:2], lexp[:, 0:1], ALU.subtract))
            link(nc.vector.tensor_scalar(nlam[:], ldif[:], -LAM_INIT, None, ALU.add))
            link(nc.vector.tensor_scalar(subg[:], subg[:], 1.0 - LAM_INIT, None, ALU.mult))

            def highest(u):
                for m in range(2):
                    dve.wait_ge(s_mm, 2 * u + m + 1)
                    link(nc.vector.tensor_reduce(top[:, m:m + 1], psS[m][:, 0:NK], AX.X, ALU.max))
                    if u >= 1:
                        dve.wait_ge(exp_done, 2 * (u - 1) + m + 1)
                    nc.vector.tensor_scalar(ntop[:, m:m + 1], top[:, m:m + 1], -SCALE, None, ALU.mult).then_inc(top_ready, 1)

            def mix(u):
                dve.wait_ge(exp_done, 2 * u + 2)
                link(nc.vector.reciprocal(inv[:], total[:]))
                link(nc.vector.tensor_tensor(coef[:], inv[:, 1:2], nlam[:], ALU.mult))
                link(nc.vector.tensor_scalar(prob[1][:], prob[1][:], coef[:, 0:1], None, ALU.mult))
                if u >= 1:
                    dve.wait_ge(t_mm, u)
                nc.vector.scalar_tensor_tensor(dif[:], prob[0][:], inv[:, 0:1], prob[1][:], ALU.mult, ALU.add).then_inc(dif_ready, 1)

            def half_copy(u):
                dve.wait_ge(t_mm, u + 1)
                if u >= 2:
                    dve.wait_ge(o_mm, u - 1)
                nc.vector.tensor_copy(probT[u % 2][:, HALF:NK], psT[:, 512:512 + NK - HALF]).then_inc(t_copied, 1)

            def finish(u):
                t, h = units[u]
                dve.wait_ge(o_mm, u + 1)
                nc.vector.tensor_copy(O[:, t, h * P:(h + 1) * P], psO[u % 2][:, 0:P]).then_inc(o_ready, 1)

            def subnorm(t):
                dve.wait_ge(o_ready, (t + 1) * CH)
                for h in range(CH):
                    cols = O[:, t, h * P:(h + 1) * P]
                    link(nc.vector.tensor_tensor_reduce(out=sq[:], in0=cols, in1=cols, scale=1.0, scalar=0.0, op0=ALU.mult, op1=ALU.add,
                                                        accum_out=oss[:, h:h + 1]))
                nc.vector.tensor_scalar(omean[:], oss[:], 1.0 / P, EPS, ALU.mult, ALU.add).then_inc(omean_ready, 1)
                dve.wait_ge(orstd_ready, t + 1)
                for h in range(CH):
                    cols = O[:, t, h * P:(h + 1) * P]
                    link(nc.vector.scalar_tensor_tensor(cols, cols, orstd[:, h:h + 1], subg[:], ALU.mult, ALU.mult))

            highest(0)
            for u in range(n_units):
                mix(u)
                if u + 1 < n_units:
                    highest(u + 1)
                if u >= 1:
                    finish(u - 1)
                    if u % CH == 0:
                        subnorm(u // CH - 1)
                half_copy(u)
            finish(n_units - 1)
            subnorm(SEQ // P - 1)

        @block.scalar
        def _(act):
            acts = [0]

            def link(ins):
                acts[0] += 1
                ins.then_inc(act_step, 1)
                act.wait_ge(act_step, acts[0])

            act.wait_ge(lsum_ready, 1)
            nc.scalar.activation(lexp[:], lsum[:], ACT.Exp).then_inc(lexp_ready, 1)

            def expo(u):
                for m in range(2):
                    act.wait_ge(top_ready, 2 * u + m + 1)
                    if u >= 1:
                        act.wait_ge(dif_ready, u)
                    nc.scalar.activation(prob[m][:], psS[m][:, 0:NK], ACT.Exp, bias=ntop[:, m:m + 1], scale=SCALE,
                                         accum_out=total[:, m:m + 1]).then_inc(exp_done, 1)

            expo(0)
            for u in range(n_units):
                if u + 1 < n_units:
                    expo(u + 1)
                if u >= 1 and u % CH == 0:
                    t = u // CH - 1
                    act.wait_ge(omean_ready, t + 1)
                    link(nc.scalar.activation(olog[:], omean[:], ACT.Ln))
                    nc.scalar.activation(orstd[:], olog[:], ACT.Exp, scale=-0.5).then_inc(orstd_ready, 1)
                act.wait_ge(t_mm, u + 1)
                if u >= 2:
                    act.wait_ge(o_mm, u - 1)
                nc.scalar.copy(probT[u % 2][:, 0:HALF], psT[:, 0:HALF]).then_inc(t_copied, 1)
            t = SEQ // P - 1
            act.wait_ge(omean_ready, t + 1)
            link(nc.scalar.activation(olog[:], omean[:], ACT.Ln))
            nc.scalar.activation(orstd[:], olog[:], ACT.Exp, scale=-0.5).then_inc(orstd_ready, 1)


def mix_out(nc, s, a, l):
    tiles = list(range(NT)) if l == 0 else list(range(CT, NT))
    with ExitStack() as ctx:
        sb = lambda n, sh, dt=F32: ctx.enter_context(nc.sbuf_tensor(f"{n}_{l}", sh, dt))
        sem = phase_semaphores(nc, ctx, f"mix_out{l}")
        ps = lambda n, w: ctx.enter_context(nc.psum_tensor(f"{n}_{l}", [P, w], F32))
        ident = sb("m_ident", [P, P])
        oT = [sb(f"m_oT{i}", [P, D]) for i in range(2)]
        sq = sb("m_sq", [P, D])
        up = sb("m_up", [P, D])
        ssq, mean, logs, rstd = (sb(f"m_{n}", [P, NT]) for n in ("ssq", "mean", "logs", "rstd"))
        psT = [ps(f"m_psT{i}", 1024) for i in range(2)]
        psY = [ps(f"m_psY{i}", 1024) for i in range(2)]
        const_in, dve_done, act_step = sem("const_in"), sem("dve_done"), sem("act_step")
        t_mm, t_copied, y_mm, mean_ready, rstd_ready, y_used = (sem(n) for n in ("t_mm", "t_copied", "y_mm", "mean_ready", "rstd_ready", "y_used"))
        block = ctx.enter_context(nc.Block())
        O = s.ho[:].rearrange("p (t n) -> p t n", t=NT)
        o0 = 0 if l == 0 else CT

        @block.sync
        def _(sp):
            sp.dma_start(ident[:], a["k_ident"]).then_inc(const_in, 16)

        @block.tensor
        def _(pe):
            pe.wait_ge(const_in, 16)

            def turn(i):
                if i >= 2:
                    pe.wait_ge(t_copied, i - 1)
                for k in range(KD):
                    tr = nc.tensor.transpose(psT[i % 2][:, k * P:(k + 1) * P], column(O[:, tiles[i] - o0, :], k), ident[:])
                tr.then_inc(t_mm, 1)

            turn(0)
            for c in range(2):
                pe.wait_ge(s.wo_in[c], 16 * (l + 1))
            for i in range(len(tiles)):
                if i + 1 < len(tiles):
                    turn(i + 1)
                pe.wait_ge(t_copied, i + 1)
                if i >= 2:
                    pe.wait_ge(y_used, i - 1)
                for c in range(2):
                    for k in range(KD):
                        mm = nc.tensor.matmul(psY[i % 2][:, c * 512:(c + 1) * 512], oT[i % 2][:, k * P:(k + 1) * P],
                                              s.ring[:, c, k * 512:(k + 1) * 512], start=(k == 0), stop=(k == KD - 1))
                mm.then_inc(y_mm, 1)

        @block.scalar
        def _(act):
            acts = [0]

            def link(ins):
                acts[0] += 1
                ins.then_inc(act_step, 1)
                act.wait_ge(act_step, acts[0])

            def copy(i):
                act.wait_ge(t_mm, i + 1)
                if i >= 2:
                    act.wait_ge(y_mm, i - 1)
                nc.scalar.copy(oT[i % 2][:], psT[i % 2][:]).then_inc(t_copied, 1)

            copy(0)
            for i in range(len(tiles)):
                if i + 1 < len(tiles):
                    copy(i + 1)
                act.wait_ge(mean_ready, i + 1)
                link(nc.scalar.activation(logs[:, i:i + 1], mean[:, i:i + 1], ACT.Ln))
                nc.scalar.activation(rstd[:, i:i + 1], logs[:, i:i + 1], ACT.Exp, scale=-0.5).then_inc(rstd_ready, 1)

        @block.vector
        def _(dve):
            chain = [0]

            def link(ins):
                chain[0] += 1
                ins.then_inc(dve_done, 1)
                dve.wait_ge(dve_done, chain[0])

            for i, t in enumerate(tiles):
                cond = 1 if t < CT else 0
                y = psY[i % 2][:]
                dve.wait_ge(y_mm, i + 1)
                link(nc.vector.tensor_copy(sq[:], y))
                link(nc.vector.tensor_tensor_reduce(out=up[:], in0=sq[:], in1=sq[:], scale=1.0, scalar=0.0, op0=ALU.mult, op1=ALU.add,
                                                    accum_out=ssq[:, i:i + 1]))
                nc.vector.tensor_scalar(mean[:, i:i + 1], ssq[:, i:i + 1], 1.0 / D, EPS, ALU.mult, ALU.add).then_inc(mean_ready, 1)
                dve.wait_ge(rstd_ready, i + 1)
                up_ins = nc.vector.scalar_tensor_tensor(up[:], sq[:], rstd[:, i:i + 1], s.bc[:, cond, 2, :], ALU.mult, ALU.mult)
                up_ins.then_inc(y_used, 1)
                dve.wait_ge(y_used, i + 1)
                link(nc.vector.tensor_tensor(s.X[:, t, :], s.X[:, t, :], up[:], ALU.add))


def route(nc, s, a, l, tiles, r):
    n_t = len(tiles)
    T = n_t * P
    with ExitStack() as ctx:
        sb = lambda n, sh, dt=F32: ctx.enter_context(nc.sbuf_tensor(f"{n}_{l}", sh, dt))
        sem = phase_semaphores(nc, ctx, f"route{l}")
        ps = lambda n, w: ctx.enter_context(nc.psum_tensor(f"{n}_{l}", [P, w], F32))
        s.bc = sb("r_bc", [P, 2, 3, D])
        zero = sb("r_zero", [P, D])
        hrow = [sb(f"r_hrow{i}", [P, D]) for i in range(2)]
        ssq, mean, logs, rstd = (sb(f"r_{n}", [P, NT]) for n in ("ssq", "mean", "logs", "rstd"))
        HT = sb("r_HT", [P, KD, T])
        rw = sb("r_rw", [P, KD, E])
        rb = sb("r_rb", [P, E])
        beforef, uptof, earlier = sb("r_beforef", [P, P]), sb("r_uptof", [P, E]), sb("r_earlier", [P, NG * NG])
        before, upto, ones = sb("r_before", [P, P], BF16), sb("r_upto", [P, E], BF16), sb("r_ones", [P, P], BF16)
        part = sb("r_part", [P, 2])
        ex, dn, sc, sel = (sb(f"r_{n}", [P, n_t, E]) for n in ("ex", "dn", "sc", "sel"))
        best = sb("r_best", [P, n_t * NG, 8])
        gs, gm, pen, rank = (sb(f"r_{n}", [P, n_t * NG]) for n in ("gs", "gm", "pen", "rank"))
        gt, eq = sb("r_gt", [P, n_t, NG, NG]), sb("r_eq", [P, n_t, NG, NG])
        msel, left, mask, wt = (sb(f"r_{n}", [P, n_t, E]) for n in ("msel", "left", "mask", "wt"))
        top8 = sb("r_top8", [P, n_t, 8])
        maskb = sb("r_maskb", [P, n_t, E], BF16)
        wsum, winv = sb("r_wsum", [P, n_t]), sb("r_winv", [P, n_t])
        res1 = sb("r_res1", [P, n_t, E])
        cmpT = sb("r_cmpT", [P, KMAX, P])
        nbT, neT = sb("r_nbT", [P, P], BF16), sb("r_neT", [P, P], BF16)
        cmp = sb("r_cmp", [P, KMAX, E])
        nb, ne = sb("r_nb", [P, E]), sb("r_ne", [P, E])
        le, lenb = sb("r_le", [P, E]), sb("r_lenb", [P, E])
        bexp, base, over, kb = (sb(f"r_{n}", [P, 1]) for n in ("bexp", "base", "over", "kb"))
        rows = sb("r_rows", [P, 3])
        order, lastord = sb("r_order", [P, 1]), sb("r_lastord", [P, 1])
        g = [sb(f"r_g{i}", [P, F]) for i in range(2)]
        ge, gd = sb("r_ge", [P, F]), sb("r_gd", [P, F])
        gT = [sb(f"r_gT{i}", [P, F]) for i in range(2)]
        ysb = [sb(f"r_y{i}", [P, D]) for i in range(2)]
        psT = ps("r_psT", 1024)
        psZ, psH, psG = ps("r_psZ", 512), ps("r_psH", 512), ps("r_psG", 512)
        psY = ps("r_psY", 1024)
        psN = ps("r_psN", 512)
        (bc_in, const_in, sh_in, dve_done, act_step, mean_ready, rstd_ready, hrow_ready, t_mm, ht_ready, z_mm, ex_ready,
         mask_ready, count_mm, nb_ready, end_mm, rows_ready, rows_mm, zero_ready, ones_ready, h_mm, e_ready, g_ready, gt_mm, gt_ready,
         y_mm, y_ready) = (
            sem(n) for n in ("bc_in", "const_in", "sh_in", "dve_done", "act_step", "mean_ready", "rstd_ready", "hrow_ready", "t_mm",
                             "ht_ready", "z_mm", "ex_ready", "mask_ready", "count_mm", "nb_ready", "end_mm", "rows_ready", "rows_mm",
                             "zero_ready", "ones_ready", "h_mm", "e_ready", "g_ready", "gt_mm", "gt_ready", "y_mm", "y_ready"))
        h_out = [sem(f"h_out{i}") for i in range(2)]
        y_out = [sem(f"y_out{i}") for i in range(2)]
        zero_out = sem("zero_out")
        block = ctx.enter_context(nc.Block())
        w13 = s.ring[:, 0, :].rearrange("p (k n) -> p k n", k=KD)
        w2 = s.ring[:, 2, :].rearrange("p (u k n) -> p u k n", u=2, k=KF)

        @block.sync
        def _(sp):
            load_modulation(nc, s, sp, l, 1, bc_in)
            for dst, src in ((r.ident[:], a["k_ident"]), (rw[:], steps(a["router_w"][l])), (rb[:], a["router_bias"][l].partition_broadcast(P)),
                             (beforef[:], a["k_before"]), (uptof[:], a["k_upto"]), (earlier[:], a["k_earlier"]), (part[:], a["k_part"]),
                             (r.slots[:], a["k_slots"])):
                sp.dma_start(dst, src).then_inc(const_in, 16)
            sp.dma_start(w13[:, :, 0:F], steps(a["sh_w1"][l])).then_inc(sh_in, 16)
            sp.dma_start(w13[:, :, F:2 * F], steps(a["sh_w3"][l])).then_inc(sh_in, 16)
            sp.dma_start(w2[:, 0, :, :], a["sh_w2"][l].rearrange("(p k) n -> p k n", k=KF)).then_inc(sh_in, 16)
            for i in range(n_t):
                sp.wait_ge(hrow_ready, i + 1)
                sp.dma_start(s.hrows[l][(i + 1) * P:(i + 2) * P, :], hrow[i % 2][:]).then_inc(h_out[i % 2], 16)
            for i in range(n_t):
                sp.wait_ge(y_ready, i + 1)
                sp.dma_start(s.yrows[l][(i + 1) * P:(i + 2) * P, :], ysb[i % 2][:]).then_inc(y_out[i % 2], 16)
            for i in range(2):
                sp.wait_ge(h_out[i], 16 * n_t // 2)
                sp.wait_ge(y_out[i], 16 * n_t // 2)

        @block.gpsimd
        def _(pool):
            nc.gpsimd.memset(zero[:], 0.0).then_inc(zero_ready, 1)
            pool.wait_ge(zero_ready, 1)
            pool.dma_start(s.hrows[l][0:P, :], zero[:]).then_inc(zero_out, 16)
            pool.dma_start(s.yrows[l][0:P, :], zero[:]).then_inc(zero_out, 16)
            pool.wait_ge(zero_out, 32)

        @block.tensor
        def _(pe):
            pe.wait_ge(const_in, 128)
            for i in range(n_t):
                pe.wait_ge(hrow_ready, i + 1)
                if i >= 1:
                    pe.wait_ge(ht_ready, i)
                for k in range(KD):
                    tr = nc.tensor.transpose(psT[:, k * P:(k + 1) * P], column(hrow[i % 2][:], k), r.ident[:])
                tr.then_inc(t_mm, 1)
                pe.wait_ge(ht_ready, i + 1)
                for k in range(KD):
                    mm = nc.tensor.matmul(psZ[:, i * E:(i + 1) * E], HT[:, k, i * P:(i + 1) * P], rw[:, k, :], start=(k == 0), stop=(k == KD - 1))
                mm.then_inc(z_mm, 1)

            def shared(i):
                if i == 0:
                    pe.wait_ge(sh_in, 48)
                if i >= 1:
                    pe.wait_ge(g_ready, i)
                for k in range(KD):
                    mm = nc.tensor.matmul(psH[:], HT[:, k, i * P:(i + 1) * P], w13[:, k, :], start=(k == 0), stop=(k == KD - 1))
                mm.then_inc(h_mm, 1)
                pe.wait_ge(g_ready, i + 1)
                if i >= 1:
                    pe.wait_ge(gt_ready, i)
                for k in range(KF):
                    tr = nc.tensor.transpose(psG[:, k * P:(k + 1) * P], g[i % 2][:].rearrange("a (p k) -> a k p", k=KF)[:, k, :], r.ident[:])
                tr.then_inc(gt_mm, 1)
                pe.wait_ge(gt_ready, i + 1)
                if i >= 1:
                    pe.wait_ge(y_ready, i)
                for c in range(2):
                    for k in range(KF):
                        mm = nc.tensor.matmul(psY[:, c * 512:(c + 1) * 512], gT[i % 2][:, k * P:(k + 1) * P], w2[:, 0, k, c * 512:(c + 1) * 512],
                                              start=(k == 0), stop=(k == KF - 1))
                mm.then_inc(y_mm, 1)

            for i in range(n_t):
                shared(i)

            pe.wait_ge(mask_ready, 1)
            pe.wait_ge(ones_ready, 1)
            for i in range(n_t):
                for j in range(i):
                    nc.tensor.matmul(psZ[:, i * E:(i + 1) * E], ones[:], maskb[:, j, :], start=(j == 0), stop=False)
                nc.tensor.matmul(psZ[:, i * E:(i + 1) * E], before[:], maskb[:, i, :], start=(i == 0), stop=True)
            for i in range(n_t):
                nc.tensor.matmul(psN[0:E, 0:P], maskb[:, i, :], ones[:], start=(i == 0), stop=(i == n_t - 1))
            for i in range(n_t):
                mm = nc.tensor.matmul(psN[:, P:P + E], ones[:], maskb[:, i, :], start=(i == 0), stop=(i == n_t - 1))
            mm.then_inc(count_mm, 1)
            pe.wait_ge(nb_ready, 1)
            nc.tensor.matmul(psN[:, 256:256 + E], nbT[0:E, :], upto[0:E, :], start=True, stop=True)
            nc.tensor.matmul(psN[:, 320:320 + E], neT[0:E, :], upto[0:E, :], start=True, stop=True).then_inc(end_mm, 1)
            pe.wait_ge(rows_ready, 1)
            for j in range(3):
                tr = nc.tensor.transpose(psG[0:1, j * P:(j + 1) * P], rows[:, j:j + 1], r.ident[:])
            tr.then_inc(rows_mm, 1)

        @block.scalar
        def _(act):
            acts = [0]

            def link(ins):
                acts[0] += 1
                ins.then_inc(act_step, 1)
                act.wait_ge(act_step, acts[0])

            act.wait_ge(mean_ready, 1)
            link(nc.scalar.activation(logs[:, 0:n_t], mean[:, 0:n_t], ACT.Ln))
            nc.scalar.activation(rstd[:, 0:n_t], logs[:, 0:n_t], ACT.Exp, scale=-0.5).then_inc(rstd_ready, 1)
            for i in range(n_t):
                act.wait_ge(t_mm, i + 1)
                nc.scalar.copy(HT[:, :, i * P:(i + 1) * P], psT[:].rearrange("p (k n) -> p k n", k=KD)).then_inc(ht_ready, 1)
            act.wait_ge(z_mm, n_t)
            nc.scalar.activation(ex[:], psZ[:, 0:n_t * E].rearrange("p (t e) -> p t e", e=E), ACT.Exp, scale=-1.0).then_inc(ex_ready, 1)
            for i in range(n_t):
                act.wait_ge(h_mm, i + 1)
                if i >= 1:
                    act.wait_ge(g_ready, i)
                nc.scalar.activation(ge[:], psH[:, 0:F], ACT.Exp, scale=-1.0).then_inc(e_ready, 1)
                act.wait_ge(gt_mm, i + 1)
                if i >= 2:
                    act.wait_ge(y_mm, i - 1)
                nc.scalar.copy(gT[i % 2][:], psG[:, 0:F]).then_inc(gt_ready, 1)
                act.wait_ge(y_mm, i + 1)
                if i >= 2:
                    act.wait_ge(y_out[i % 2], 16 * (i // 2))
                nc.scalar.copy(ysb[i % 2][:], psY[:]).then_inc(y_ready, 1)

        @block.vector
        def _(dve):
            chain = [0]

            def link(ins):
                chain[0] += 1
                ins.then_inc(dve_done, 1)
                dve.wait_ge(dve_done, chain[0])

            for i, t in enumerate(tiles):
                link(nc.vector.tensor_tensor_reduce(out=hrow[0][:], in0=s.X[:, t, :], in1=s.X[:, t, :], scale=1.0, scalar=0.0,
                                                    op0=ALU.mult, op1=ALU.add, accum_out=ssq[:, i:i + 1]))
            nc.vector.tensor_scalar(mean[:, 0:n_t], ssq[:, 0:n_t], 1.0 / D, EPS, ALU.mult, ALU.add).then_inc(mean_ready, 1)
            dve.wait_ge(bc_in, 32)
            dve.wait_ge(rstd_ready, 1)
            for i, t in enumerate(tiles):
                cond = 1 if t < CT else 0
                if i >= 2:
                    dve.wait_ge(t_mm, i - 1)
                    dve.wait_ge(h_out[i % 2], 16 * (i // 2))
                link(nc.vector.scalar_tensor_tensor(hrow[i % 2][:], s.X[:, t, :], rstd[:, i:i + 1], s.bc[:, cond, 1, :], ALU.mult, ALU.mult))
                nc.vector.tensor_tensor(hrow[i % 2][:], hrow[i % 2][:], s.bc[:, cond, 0, :], ALU.add).then_inc(hrow_ready, 1)
            dve.wait_ge(const_in, 128)
            link(nc.vector.tensor_copy(before[:], beforef[:]))
            link(nc.vector.tensor_copy(upto[:], uptof[:]))
            nc.vector.memset(ones[:], 1.0).then_inc(ones_ready, 1)

            def shared_gate(i):
                b = i % 2
                dve.wait_ge(e_ready, i + 1)
                link(nc.vector.tensor_scalar(ge[:], ge[:], 1.0, None, ALU.add))
                link(nc.vector.reciprocal(gd[:], ge[:]))
                link(nc.vector.tensor_tensor(gd[:], gd[:], psH[:, 0:F], ALU.mult))
                if i >= 2:
                    dve.wait_ge(gt_mm, i - 1)
                nc.vector.tensor_tensor(g[b][:], gd[:], psH[:, F:2 * F], ALU.mult).then_inc(g_ready, 1)

            shared_gate(0)
            dve.wait_ge(ex_ready, 1)
            link(nc.vector.tensor_scalar(dn[:], ex[:], 1.0, None, ALU.add))
            link(nc.vector.reciprocal(sc[:], dn[:]))
            link(nc.vector.tensor_tensor(sel[:], sc[:], rb[:].unsqueeze(1).to_broadcast([P, n_t, E]), ALU.add))
            flat = sel[:].rearrange("p t (g e) -> p (t g) e", e=EG)
            for j in range(n_t * NG):
                last = nc.vector.max(best[:, j, :], flat[:, j, :])
                if j % NG == NG - 1:
                    link(last)
                if j == 3 * NG - 1:
                    shared_gate(1)
            link(nc.vector.tensor_tensor(gs[:], best[:, :, 0], best[:, :, 1], ALU.add))
            if n_t > 2:
                shared_gate(2)
            g3 = gs[:].rearrange("p (t g) -> p t g", g=NG)
            theirs = g3.unsqueeze(2).to_broadcast([P, n_t, NG, NG])
            own = g3.unsqueeze(3).to_broadcast([P, n_t, NG, NG])
            link(nc.vector.tensor_tensor(gt[:], theirs, own, ALU.is_gt))
            link(nc.vector.tensor_tensor(eq[:], theirs, own, ALU.is_equal))
            eqf, gtf = eq[:].rearrange("p t i j -> p t (i j)"), gt[:].rearrange("p t i j -> p t (i j)")
            link(nc.vector.tensor_tensor(eqf, eqf, earlier[:].unsqueeze(1).to_broadcast([P, n_t, NG * NG]), ALU.mult))
            link(nc.vector.tensor_tensor(gtf, gtf, eqf, ALU.add))
            link(nc.vector.tensor_reduce(rank[:], gt[:].rearrange("p t i j -> p (t i) j"), AX.X, ALU.add))
            link(nc.vector.tensor_scalar(gm[:], rank[:], float(TOPG), None, ALU.is_lt))
            link(nc.vector.tensor_scalar(pen[:], gm[:], -1.0, -NEG, ALU.add, ALU.mult))
            mflat = msel[:].rearrange("p t (g e) -> p (t g) e", e=EG)
            link(nc.vector.tensor_tensor(mflat, flat, gm[:].unsqueeze(2).to_broadcast([P, n_t * NG, EG]), ALU.mult))
            link(nc.vector.tensor_tensor(mflat, mflat, pen[:].unsqueeze(2).to_broadcast([P, n_t * NG, EG]), ALU.add))
            if n_t > 3:
                shared_gate(3)
            for i in range(n_t):
                link(nc.vector.max(top8[:, i, :], msel[:, i, :]))
                link(nc.vector.match_replace(left[:, i, :], top8[:, i, :], msel[:, i, :], -3e38))
            link(nc.vector.tensor_scalar(mask[:], left[:], -2e38, None, ALU.is_lt))
            nc.vector.tensor_copy(maskb[:], mask[:]).then_inc(mask_ready, 1)
            link(nc.vector.tensor_tensor(wt[:], sc[:], mask[:], ALU.mult))
            link(nc.vector.tensor_reduce(wsum[:], wt[:], AX.X, ALU.add))
            link(nc.vector.reciprocal(winv[:], wsum[:]))
            link(nc.vector.tensor_tensor(wt[:], wt[:], winv[:].unsqueeze(2).to_broadcast([P, n_t, E]), ALU.mult))
            link(nc.vector.tensor_scalar(wt[:], wt[:], ROUTED_SCALE, None, ALU.mult))
            for i in range(4, n_t):
                shared_gate(i)
            link(nc.vector.tensor_copy(r.tab5[:, :, :, 0], wt[:]))
            link(nc.vector.tensor_tensor(res1[:], wt[:], r.tab5[:, :, :, 0], ALU.subtract))
            link(nc.vector.tensor_copy(r.tab5[:, :, :, 1], res1[:]))
            link(nc.vector.tensor_tensor(res1[:], res1[:], r.tab5[:, :, :, 1], ALU.subtract))
            link(nc.vector.tensor_copy(r.tab5[:, :, :, 2], res1[:]))
            for i in range(n_t):
                link(nc.vector.memset(r.tab5[:, i, :, 3], float((i + 1) * P)))
            link(nc.vector.tensor_copy(r.tab5[:, :, :, 4], part[:, 0:1].unsqueeze(2).to_broadcast([P, n_t, E])))
            link(nc.vector.tensor_copy(r.spare[:], part[:, 0:1]))
            dve.wait_ge(count_mm, 1)
            pos = psZ[:, 0:n_t * E].rearrange("p (t e) -> p t e", e=E)
            link(nc.vector.scalar_tensor_tensor(res1[:], pos, 1.0, mask[:], ALU.add, ALU.mult))
            link(nc.vector.tensor_scalar(r.posm[:].rearrange("p e t -> p t e"), res1[:], -1.0, None, ALU.add))
            for j in range(KMAX):
                link(nc.vector.tensor_scalar(cmpT[0:E, j, :], psN[0:E, 0:P], float(j * P), None, ALU.is_gt))
                link(nc.vector.tensor_scalar(cmp[:, j, :], psN[:, P:P + E], float(j * P), None, ALU.is_gt))
            link(nc.vector.tensor_copy(neT[0:E, :], cmpT[0:E, 0, :]))
            with nc.allow_low_precision("counts up to 6 are exact"):
                nc.vector.tensor_reduce(nbT[0:E, :], cmpT[0:E].rearrange("p j n -> p n j"), AX.X, ALU.add).then_inc(nb_ready, 1)
            link(nc.vector.tensor_reduce(nb[:], cmp[:].rearrange("p j n -> p n j"), AX.X, ALU.add))
            dve.wait_ge(end_mm, 1)
            end, used = psN[:, 256:256 + E], psN[:, 320:320 + E]
            link(nc.vector.tensor_scalar(le[:], end, part[:, 0:1], None, ALU.is_le))
            link(nc.vector.tensor_tensor(lenb[:], le[:], nb[:], ALU.mult))
            link(nc.vector.tensor_reduce(bexp[:], le[:], AX.X, ALU.add))
            link(nc.vector.tensor_reduce(base[:], lenb[:], AX.X, ALU.add))
            link(nc.vector.tensor_tensor(lenb[:], le[:], cmp[:, 0, :], ALU.mult))
            link(nc.vector.tensor_reduce(order[:], lenb[:], AX.X, ALU.add))
            link(nc.vector.tensor_scalar(lastord[:], used[:, E - 1:E], -1.0, None, ALU.add))
            link(nc.vector.tensor_scalar(over[:], bexp[:], float(E), float(KMAX), ALU.is_ge, ALU.mult))
            link(nc.vector.tensor_tensor(kb[:], part[:, 0:1], base[:], ALU.subtract))
            link(nc.vector.tensor_tensor(kb[:], kb[:], over[:], ALU.add))
            link(nc.vector.tensor_scalar(rows[:, 0:1], bexp[:], float(E - 1), None, ALU.min))
            link(nc.vector.tensor_scalar(kb[:], kb[:], float(KMAX), None, ALU.min))
            link(nc.vector.tensor_tensor(order[:], order[:], lastord[:], ALU.min))
            link(nc.vector.scalar_tensor_tensor(kb[:], order[:], 8.0, kb[:], ALU.mult, ALU.add))
            link(nc.vector.scalar_tensor_tensor(rows[:, 1:2], rows[:, 0:1], 8.0 * E, kb[:], ALU.mult, ALU.add))
            link(nc.vector.tensor_scalar(ne[:], used, part[:, 0:1], None, ALU.is_le))
            link(nc.vector.tensor_reduce(bexp[:], ne[:], AX.X, ALU.add))
            nc.vector.tensor_scalar(rows[:, 2:3], bexp[:], float(E - 1), None, ALU.min).then_inc(rows_ready, 1)
            last = 3 * P
            link(nc.vector.tensor_copy(r.table[0:1, last:last + 1], end[0:1, E - 1:E]))
            link(nc.vector.tensor_scalar(r.table[0:1, last + 1:last + 2], used[0:1, E - 1:E], 1.0, None, ALU.add))
            link(nc.vector.tensor_scalar(r.table[0:1, last + 2:last + 4], r.table[0:1, last:last + 2], 1, None, ALU.logical_shift_right))
            link(nc.vector.tensor_scalar(r.table[0:1, last + 4:last + 5], r.table[0:1, last + 2:last + 3], 2.0, -2.0, ALU.mult, ALU.add))
            dve.wait_ge(rows_mm, 1)
            link(nc.vector.tensor_copy(r.table[0:1, 0:last], psG[0:1, 0:last]))


def wait_for(eng, sem, value):
    if not isinstance(value, int) or value > 0:
        eng.wait_ge(sem, value)


def experts(nc, s, a, l, n_t, r):
    T = n_t * P
    PIECE = 4
    KP = KD // PIECE
    last = 3 * P
    w1 = a["exp_w1"][l].rearrange("e (p k) n -> e p (k n)", p=P)
    w3 = a["exp_w3"][l].rearrange("e (p k) n -> e p (k n)", p=P)
    w2 = a["exp_w2"][l].rearrange("e (p k) n -> e p (k n)", k=KF)
    with ExitStack() as ctx:
        sb = lambda n, sh, dt=F32: ctx.enter_context(nc.sbuf_tensor(f"{n}_{l}", sh, dt))
        sem = phase_semaphores(nc, ctx, f"experts{l}")
        ps = lambda n, w: ctx.enter_context(nc.psum_tensor(f"{n}_{l}", [P, w], F32))
        w13h, w13l = (sb(f"e_w13{n}", [P, 2, 2, KD, F], F32R) for n in "hl")
        w2h, w2l = (sb(f"e_w2{n}", [P, KF, D], F32R) for n in "hl")
        xg = [sb(f"e_xg{i}", [P, D]) for i in range(2)]
        xh, xl = ([sb(f"e_x{n}{i}", [P, D], F32R) for i in range(2)] for n in "hl")
        sel = [sb(f"e_sel{i}", [P, n_t, P], BF16) for i in range(2)]
        gidx = [sb(f"e_gidx{i}", [P, 1], U32) for i in range(2)]
        gw = [sb(f"e_gw{i}", [P, 1]) for i in range(2)]
        sidx = [sb(f"e_sidx{i}", [P, 1], U32) for i in range(2)]
        sw = [sb(f"e_sw{i}", [P, 1]) for i in range(2)]
        tok = sb("e_tok", [P, 1])
        ge, hh, g = sb("e_ge", [P, F]), sb("e_hh", [P, F]), sb("e_g", [P, F])
        gh, gl = ([sb(f"e_g{n}{i}", [P, F], F32R) for i in range(2)] for n in "hl")
        ysb = [sb(f"e_y{i}", [P, D]) for i in range(2)]
        psT, psY = ps("e_psT", 1024), ps("e_psY", 1024)
        psH = [ps(f"e_psH{i}", 512) for i in range(2)]
        psG, psI = ps("e_psG", 512), ps("e_psI", 512)
        gathered = [sem(f"gathered{i}") for i in range(2)]
        (w13_in, w2_in, w13_hi, w13_lo, w2_hi, w2_lo, sel_ready, idx_mm, idx_step, idx_ready, copied, xt_mm, x_hi, x_lo, h_mm,
         e_ready, g_step, g_ready, gt_mm, g_hi, g_lo, y_mm, y_ready, added, pool_clear, sp_clear) = (sem(n) for n in (
             "w13_in", "w2_in", "w13_hi", "w13_lo", "w2_hi", "w2_lo", "sel_ready", "idx_mm", "idx_step", "idx_ready", "copied",
             "xt_mm", "x_hi", "x_lo", "h_mm", "e_ready", "g_step", "g_ready", "gt_mm", "g_hi", "g_lo", "y_mm", "y_ready",
             "added", "pool_clear", "sp_clear"))
        block = ctx.enter_context(nc.Block())
        raw13 = s.ring[:, 0:2, :].rearrange("p o (u k n) -> p o u k n", u=2, n=F)
        raw2 = s.ring[:, 2, :].rearrange("p (o k n) -> p o k n", o=2, k=KF)

        def entry(eng, row, b, top):
            return eng.value_load(r.table[0:1, bass.DynSlice(b + row * P, 1)], min_val=0, max_val=top)

        expert_of = lambda eng, b: entry(eng, 0, b, E - 1)
        code_of = lambda eng, b: entry(eng, 1, b, 8 * E * E - 1)
        order_in = lambda code: (code >> 3) & (E - 1)
        half_in = lambda code: (code >> 3) & 1
        expert_in = lambda code: (code >> 9).with_bounds(min_val=0, max_val=E - 1)
        expert_at = lambda eng, o: entry(eng, 2, o, E - 1)
        pairs = lambda eng: eng.value_load(r.table[0:1, last + 2:last + 3], min_val=2, max_val=(P - 6) // 2)
        ending = lambda eng: eng.value_load(r.table[0:1, last + 4:last + 5], min_val=2, max_val=P - 8)

        @block.sync
        def _(sp):
            def load13(o, par):
                e = expert_at(sp, o)
                wait_for(sp, w13_in, 32 * o)
                sp.sem_inc(sp_clear, 1)
                wait_for(sp, w13_lo, PIECE * (o - 1))
                for u, w in enumerate((w1, w3)):
                    sp.dma_start(s.ring[:, par, u * KD * F:(u + 1) * KD * F].unsqueeze(1),
                                 w[bass.DynSlice(e, 1)].rearrange("e p n -> p e n")).then_inc(w13_in, 16)

            def load2(o, par):
                e = expert_at(sp, o)
                wait_for(sp, w2_in, 16 * o)
                sp.sem_inc(sp_clear, 1)
                wait_for(sp, w2_lo, 2 * (o - 1))
                sp.dma_start(s.ring[:, 2, par * KF * D:(par + 1) * KF * D].unsqueeze(1),
                             w2[bass.DynSlice(e, 1)].rearrange("e p n -> p e n")).then_inc(w2_in, 16)

            n = sp.value_load(r.table[0:1, last + 3:last + 4], min_val=4, max_val=E // 2)
            load13(0, 0)

            def pair(i):
                load13(2 * i + 1, 1)
                load2(2 * i, 0)
                load13(2 * i + 2, 0)
                load2(2 * i + 1, 1)

            pair(0)
            with sp.Fori(0, n - 1) as i:
                pair(i + 1)
            sp.wait_ge(w13_in, 64 * n + 32)
            sp.sem_inc(sp_clear, 1)
            sp.wait_ge(w2_in, 32 * n)
            sp.sem_inc(sp_clear, 1)

        @block.gpsimd
        def _(pool):
            def gather(b, par):
                pool.wait_ge(idx_ready, b + 1)
                wait_for(pool, xt_mm, 2 * (b - 1))
                pool.sem_inc(pool_clear, 1)
                nc.gpsimd.indirect_dma_start(xg[par][:], None, s.hrows[l], bass.IndirectOffsetOnAxis(ap=gidx[par][:, 0:1], axis=0)
                                             ).then_inc(gathered[par], 16)

            def scatter(b, par):
                if isinstance(b, int) and b < 0:
                    return
                pool.wait_ge(copied, 2 * b + 2)
                pool.wait_ge(y_ready, b + 1)
                wait_for(pool, added, 16 * b)
                pool.sem_inc(pool_clear, 1)
                nc.gpsimd.indirect_dma_start(s.yrows[l], bass.IndirectOffsetOnAxis(ap=sidx[par][:, 0:1], axis=0), ysb[par][:], None,
                                             compute_op=ALU.add).then_inc(added, 16)

            def keep(b, par):
                wait_for(pool, added, 16 * (b - 1))
                pool.sem_inc(pool_clear, 1)
                nc.gpsimd.tensor_copy(sidx[par][:], gidx[par][:]).then_inc(copied, 1)
                nc.gpsimd.tensor_copy(sw[par][:], gw[par][:]).then_inc(copied, 1)

            def step(b, par):
                keep(b, par)
                gather(b + 2, par)
                scatter(b - 1, 1 - par)

            n = pairs(pool)
            gather(0, 0)
            gather(1, 1)
            step(0, 0)
            step(1, 1)
            step(2, 0)
            with pool.Fori(0, n - 1) as i:
                step(2 * i + 3, 1)
                step(2 * i + 4, 0)
            m = ending(pool)
            scatter(m + 2, 0)
            pool.wait_ge(added, 16 * (2 * n + 1))
            pool.wait_ge(gathered[0], 16 * (n + 2))
            pool.wait_ge(gathered[1], 16 * (n + 1))

        @block.tensor
        def _(pe):
            def index(b, par):
                e = expert_of(pe, b)
                pe.wait_ge(sel_ready, b + 1)
                wait_for(pe, idx_ready, b)
                for t in range(n_t):
                    mm = nc.tensor.matmul(psI[:, 0:5], sel[par][:, t, :], r.tab5[:, t, bass.DynSlice(e, 1), :],
                                          start=(t == 0), stop=(t == n_t - 1))
                mm.then_inc(idx_mm, 1)

            def turn(b, m, par):
                pe.wait_ge(gathered[par], 16 * m + 16)
                wait_for(pe, x_lo, 2 * b)
                for k in range(KD):
                    tr = nc.tensor.transpose(psT[:, k * P:(k + 1) * P], column(xg[par][:], k), r.ident[:])
                    if k == KD // 2 - 1:
                        tr.then_inc(xt_mm, 1)
                tr.then_inc(xt_mm, 1)

            def hidden(b, par):
                code = code_of(pe, b)
                o, half = order_in(code), half_in(code)
                wait_for(pe, g_ready, b - 1)
                for k in range(KD):
                    if k % (KD // 2) == 0:
                        pe.wait_ge(x_hi, 2 * b + 1 + k // (KD // 2))
                    if k % KP == 0:
                        pe.wait_ge(w13_lo, PIECE * o + k // KP + 1)
                    for i, w in enumerate((w13h, w13l)):
                        nc.tensor.matmul(psH[par][:], xh[par][:, k * P:(k + 1) * P], w[:, bass.DynSlice(half, 1), :, k, :],
                                         start=(k == 0 and i == 0), stop=False)
                for k in range(KD):
                    if k % (KD // 2) == 0:
                        pe.wait_ge(x_lo, 2 * b + 1 + k // (KD // 2))
                    mm = nc.tensor.matmul(psH[par][:], xl[par][:, k * P:(k + 1) * P], w13h[:, bass.DynSlice(half, 1), :, k, :],
                                          start=False, stop=(k == KD - 1))
                mm.then_inc(h_mm, 1)

            def turn_gate(b):
                pe.wait_ge(g_ready, b + 1)
                wait_for(pe, g_lo, b)
                for k in range(KF):
                    tr = nc.tensor.transpose(psG[:, k * P:(k + 1) * P], g[:].rearrange("a (p k) -> a k p", k=KF)[:, k, :], r.ident[:])
                tr.then_inc(gt_mm, 1)

            def down(b, par):
                o = order_in(code_of(pe, b))
                pe.wait_ge(g_hi, b + 1)
                wait_for(pe, y_ready, b)
                for k in range(KF):
                    pe.wait_ge(w2_lo, 2 * o + k + 1)
                    for c in range(2):
                        for i, w in enumerate((w2h, w2l)):
                            nc.tensor.matmul(psY[:, c * 512:(c + 1) * 512], gh[par][:, k * P:(k + 1) * P], w[:, k, c * 512:(c + 1) * 512],
                                             start=(k == 0 and i == 0), stop=False)
                pe.wait_ge(g_lo, b + 1)
                for k in range(KF):
                    for c in range(2):
                        mm = nc.tensor.matmul(psY[:, c * 512:(c + 1) * 512], gl[par][:, k * P:(k + 1) * P], w2h[:, k, c * 512:(c + 1) * 512],
                                              start=False, stop=(k == KF - 1))
                mm.then_inc(y_mm, 1)

            n = pairs(pe)
            index(0, 0)
            index(1, 1)
            turn(0, 0, 0)
            hidden(0, 0)
            index(2, 0)
            turn(1, 0, 1)

            def pair(i):
                hidden(2 * i + 1, 1)
                index(2 * i + 3, 1)
                turn_gate(2 * i)
                turn(2 * i + 2, i + 1, 0)
                down(2 * i, 0)
                hidden(2 * i + 2, 0)
                index(2 * i + 4, 0)
                turn_gate(2 * i + 1)
                turn(2 * i + 3, i + 1, 1)
                down(2 * i + 1, 1)

            pair(0)
            with pe.Fori(0, n - 1) as i:
                pair(i + 1)
            turn_gate(2 * n)
            down(2 * n, 0)

        @block.scalar
        def _(act):
            def split2(b):
                code = code_of(act, b)
                with act.If((code & 7) == 0):
                    o, half = order_in(code), half_in(code)
                    act.wait_ge(w2_in, 16 * o + 16)
                    wait_for(act, y_mm, b)
                    for k in range(KF):
                        nc.scalar.copy(w2h[:, k:k + 1, :], raw2[:, bass.DynSlice(half, 1), k, :]).then_inc(w2_hi, 1)

            def split13(b, pieces):
                code = code_of(act, b)
                with act.If((code & 7) == 0):
                    o, half = order_in(code), half_in(code)
                    act.wait_ge(w13_in, 32 * o + 32)
                    wait_for(act, h_mm, b - 1)
                    for j in pieces:
                        k = slice(j * KP, (j + 1) * KP)
                        nc.scalar.copy(w13h[:, bass.DynSlice(half, 1), :, k, :].rearrange("p o u k n -> p (o u) (k n)"),
                                       raw13[:, bass.DynSlice(half, 1), :, k, :].rearrange("p o u k n -> p (o u) (k n)")).then_inc(w13_hi, 1)

            def expo(b, par):
                act.wait_ge(h_mm, b + 1)
                wait_for(act, g_step, b)
                nc.scalar.activation(ge[:], psH[par][:, 0:F], ACT.Sigmoid).then_inc(e_ready, 1)

            def gate(b, par):
                if isinstance(b, int) and b < 0:
                    return
                act.wait_ge(gt_mm, b + 1)
                wait_for(act, y_mm, b - 1)
                nc.scalar.copy(gh[par][:], psG[:, 0:F]).then_inc(g_hi, 1)

            def rows_in(b, par):
                wait_for(act, h_mm, b - 1)
                for j in range(2):
                    act.wait_ge(xt_mm, 2 * b + 1 + j)
                    nc.scalar.copy(xh[par][:, j * 512:(j + 1) * 512], psT[:, j * 512:(j + 1) * 512]).then_inc(x_hi, 1)

            def rows_out(b, par):
                if isinstance(b, int) and b < 0:
                    return
                act.wait_ge(y_mm, b + 1)
                act.wait_ge(copied, 2 * b + 2)
                wait_for(act, added, 16 * (b - 1))
                nc.scalar.activation(ysb[par][:], psY[:], ACT.Copy, scale=sw[par][:, 0:1]).then_inc(y_ready, 1)

            def step(b, par):
                expo(b, par)
                gate(b - 1, 1 - par)
                rows_in(b + 1, 1 - par)
                split13(b + 2, range(PIECE))
                rows_out(b - 1, 1 - par)
                split2(b)

            n = pairs(act)
            split13(0, range(PIECE))
            rows_in(0, 0)
            split13(1, range(PIECE))
            step(0, 0)
            step(1, 1)
            step(2, 0)
            with act.Fori(0, n - 1) as i:
                step(2 * i + 3, 1)
                step(2 * i + 4, 0)
            m = ending(act)
            gate(m + 2, 0)
            rows_out(m + 2, 0)

        @block.vector
        def _(dve):
            def choose(b, par):
                code = code_of(dve, b)
                e, at = expert_in(code), ((code & 7) * P).with_bounds(min_val=0, max_val=KMAX * P)
                wait_for(dve, idx_mm, b - 1)
                nc.vector.tensor_tensor(sel[par][:], r.slots[:, bass.DynSlice(at, P)].unsqueeze(1).to_broadcast([P, n_t, P]),
                                        r.posm[:, bass.DynSlice(e, 1), :].rearrange("p e t -> p t e").to_broadcast([P, n_t, P]),
                                        ALU.is_equal).then_inc(sel_ready, 1)

            def indices(b, par):
                dve.wait_ge(idx_mm, b + 1)
                wait_for(dve, copied, 2 * (b - 1))
                nc.vector.tensor_reduce(tok[:], psI[:, 3:5], AX.X, ALU.add).then_inc(idx_step, 1)
                nc.vector.tensor_reduce(gw[par][:], psI[:, 0:3], AX.X, ALU.add).then_inc(idx_step, 1)
                dve.wait_ge(idx_step, 2 * b + 2)
                nc.vector.tensor_scalar(gidx[par][:], tok[:], r.spare[:, 0:1], None, ALU.max).then_inc(idx_ready, 1)

            def rest2(b):
                code = code_of(dve, b)
                with dve.If((code & 7) == 0):
                    o, half = order_in(code), half_in(code)
                    for k in range(KF):
                        dve.wait_ge(w2_hi, 2 * o + k + 1)
                        nc.vector.tensor_tensor(w2l[:, k:k + 1, :], raw2[:, bass.DynSlice(half, 1), k, :], w2h[:, k:k + 1, :].bitcast(F32),
                                                ALU.subtract).then_inc(w2_lo, 1)

            def rest13(b, pieces):
                code = code_of(dve, b)
                with dve.If((code & 7) == 0):
                    o, half = order_in(code), half_in(code)
                    for j in pieces:
                        k = slice(j * KP, (j + 1) * KP)
                        dve.wait_ge(w13_hi, PIECE * o + j + 1)
                        raw, high, low = (x[:, bass.DynSlice(half, 1), :, k, :].rearrange("p o u k n -> p (o u) (k n)")
                                          for x in (raw13, w13h, w13l))
                        nc.vector.tensor_tensor(low, raw, high.bitcast(F32), ALU.subtract).then_inc(w13_lo, 1)

            def gate(b, par):
                if isinstance(b, int) and b < 0:
                    return
                dve.wait_ge(g_hi, b + 1)
                nc.vector.tensor_tensor(gl[par][:], psG[:, 0:F], gh[par][:].bitcast(F32), ALU.subtract).then_inc(g_lo, 1)

            def rows_in(b, par):
                for j in range(2):
                    dve.wait_ge(x_hi, 2 * b + 1 + j)
                    c = slice(j * 512, (j + 1) * 512)
                    nc.vector.tensor_tensor(xl[par][:, c], psT[:, c], xh[par][:, c].bitcast(F32), ALU.subtract).then_inc(x_lo, 1)

            def silu(b, par):
                dve.wait_ge(e_ready, b + 1)
                nc.vector.tensor_tensor(hh[:], ge[:], psH[par][:, 0:F], ALU.mult).then_inc(g_step, 1)
                dve.wait_ge(g_step, b + 1)
                wait_for(dve, gt_mm, b)
                nc.vector.tensor_tensor(g[:], hh[:], psH[par][:, F:2 * F], ALU.mult).then_inc(g_ready, 1)

            def step(b, par):
                gate(b - 1, 1 - par)
                indices(b + 2, par)
                rows_in(b + 1, 1 - par)
                silu(b, par)
                choose(b + 3, 1 - par)
                rest13(b + 2, range(PIECE))
                rest2(b)

            n = pairs(dve)
            choose(0, 0)
            indices(0, 0)
            choose(1, 1)
            indices(1, 1)
            choose(2, 0)
            rest13(0, range(PIECE))
            rows_in(0, 0)
            rest13(1, range(PIECE))
            step(0, 0)
            step(1, 1)
            step(2, 0)
            with dve.Fori(0, n - 1) as i:
                step(2 * i + 3, 1)
                step(2 * i + 4, 0)
            gate(2 * n, 0)


def combine(nc, s, a, l, tiles):
    last = l == DEPTH - 1
    with ExitStack() as ctx:
        sb = lambda n, sh, dt=F32: ctx.enter_context(nc.sbuf_tensor(f"{n}_{l}", sh, dt))
        sem = phase_semaphores(nc, ctx, f"combine{l}")
        gate = sb("f_gate", [P, 2, D])
        Y = sb("f_Y", [P, len(tiles), D])
        up = sb("f_up", [P, D])
        ssq, mean, logs, rstd = (sb(f"f_{n}", [P, NT]) for n in ("ssq", "mean", "logs", "rstd"))
        y_in = [sem(f"y_in{i}") for i in range(len(tiles))]
        gate_in, dve_done, act_step, mean_ready, rstd_ready, x_ready, out_done = (
            sem(n) for n in ("gate_in", "dve_done", "act_step", "mean_ready", "rstd_ready", "x_ready", "out_done"))
        block = ctx.enter_context(nc.Block())

        @block.sync
        def _(sp):
            for cond in range(2):
                sp.dma_start(gate[:, cond, :], s.mod[l, cond, 5, :].partition_broadcast(P)).then_inc(gate_in, 16)
            for i in range(len(tiles)):
                sp.dma_start(Y[:, i, :], s.yrows[l][(i + 1) * P:(i + 2) * P, :]).then_inc(y_in[i], 16)
            if last:
                out = a["out"].rearrange("o (t p) d -> (o t) p d", p=P)
                for i in range(len(tiles)):
                    sp.wait_ge(x_ready, i + 1)
                    sp.dma_start(out[i], s.X[:, tiles[i], :]).then_inc(out_done, 16)
                sp.wait_ge(out_done, 16 * len(tiles))

        @block.scalar
        def _(act):
            for i in range(len(tiles)):
                act.wait_ge(mean_ready, i + 1)
                nc.scalar.activation(logs[:, i:i + 1], mean[:, i:i + 1], ACT.Ln).then_inc(act_step, 1)
                act.wait_ge(act_step, i + 1)
                nc.scalar.activation(rstd[:, i:i + 1], logs[:, i:i + 1], ACT.Exp, scale=-0.5).then_inc(rstd_ready, 1)

        @block.vector
        def _(dve):
            chain = [0]

            def link(ins):
                chain[0] += 1
                ins.then_inc(dve_done, 1)
                dve.wait_ge(dve_done, chain[0])

            def square(i):
                dve.wait_ge(y_in[i], 16)
                link(nc.vector.tensor_tensor_reduce(out=up[:], in0=Y[:, i, :], in1=Y[:, i, :], scale=1.0, scalar=0.0, op0=ALU.mult,
                                                    op1=ALU.add, accum_out=ssq[:, i:i + 1]))
                nc.vector.tensor_scalar(mean[:, i:i + 1], ssq[:, i:i + 1], 1.0 / D, EPS, ALU.mult, ALU.add).then_inc(mean_ready, 1)

            square(0)
            dve.wait_ge(gate_in, 32)
            for i, t in enumerate(tiles):
                if i + 1 < len(tiles):
                    square(i + 1)
                cond = 1 if t < CT else 0
                dve.wait_ge(rstd_ready, i + 1)
                link(nc.vector.scalar_tensor_tensor(Y[:, i, :], Y[:, i, :], rstd[:, i:i + 1], gate[:, cond, :], ALU.mult, ALU.mult))
                nc.vector.tensor_tensor(s.X[:, t, :], s.X[:, t, :], Y[:, i, :], ALU.add).then_inc(x_ready, 1)
                dve.wait_ge(x_ready, i + 1)


def hybrid_backbone(nc, a, stop=None):
    with ExitStack() as top:
        s = Core()
        s.X = top.enter_context(nc.sbuf_tensor("X", [P, NT, D], F32))
        s.ring = top.enter_context(nc.sbuf_tensor("ring", [P, RING, 4096], F32))
        s.mod = nc.dram_tensor("mod_rows", [DEPTH, 2, 6, D], F32, kind="Internal").ap()
        s.hrows = [nc.dram_tensor(f"h_rows{l}", [(NTOK if l == 0 else SEQ) + P, D], F32, kind="Internal").ap() for l in range(DEPTH)]
        s.yrows = [nc.dram_tensor(f"y_rows{l}", [(NTOK if l == 0 else SEQ) + P, D], F32, kind="Internal").ap() for l in range(DEPTH)]
        s.x_in = top.enter_context(nc.semaphore("x_in"))
        s.wo_in = [top.enter_context(nc.semaphore(f"wo_in{i}")) for i in range(2)]
        adaln(nc, s, a)
        for l in range(DEPTH):
            with ExitStack() as mixer:
                sb = lambda n, sh: mixer.enter_context(nc.sbuf_tensor(f"{n}_{l}", sh, F32))
                s.bc = sb("bc", [P, 2, 3, D])
                s.ho = sb("ho", [P, NT * D])
                qt = sb("qt", [P, 8, NTOK if l == 0 else SEQ])
                kt = sb("kt", [P, 2 if l == 0 else CH, NTOK])
                v = sb("v", [P, NT, 2 * GROUPS_KV * HD if l == 0 else D])
                project(nc, s, a, l, qt, kt, v)
                (attend_ab if l == 0 else attend_c)(nc, s, a, qt, kt, v)
                mix_out(nc, s, a, l)
            tiles = list(range(NT)) if l == 0 else list(range(CT, NT))
            with ExitStack() as moe:
                sb = lambda n, sh, dt=F32: moe.enter_context(nc.sbuf_tensor(f"{n}_{l}", sh, dt))
                r = Core()
                n_t = len(tiles)
                r.ident = sb("m_id", [P, P])
                r.slots = sb("slots", [P, P * (KMAX + 1)])
                r.tab5 = sb("tab5", [P, n_t, E, 5], BF16)
                r.posm = sb("posm", [P, E, n_t])
                r.spare = sb("spare", [P, 1])
                r.table = sb("table", [1, 3 * P + 5], I32)
                route(nc, s, a, l, tiles, r)
                experts(nc, s, a, l, n_t, r)
            combine(nc, s, a, l, tiles)


_INS = ["x", "c", "ctx", "c_ctx", "ada_w", "ada_b", "norm_g", "ab_w_in", "ab_w_out", "a_q_norm", "a_k_norm", "b_sink", "c_w_in",
        "c_w_out", "c_lambda", "c_subln_g", "router_w", "router_bias", "exp_w1", "exp_w3", "exp_w2", "sh_w1", "sh_w3", "sh_w2"]


def kernel(**inputs):
    import concourse.bacc as bacc
    from concourse.bass_utils import run_bass_kernel_spmd

    nc = bacc.Bacc("TRN2", target_bir_lowering=False, num_devices=1)
    arrays, aps = {}, {}
    for name, value in [(n, inputs[n]) for n in _INS] + list(host_constants().items()):
        v = np.ascontiguousarray(value)
        arrays[f"in_{name}"] = v
        aps[name] = nc.dram_tensor(f"in_{name}", v.shape, mybir.dt.from_np(v.dtype), kind="ExternalInput").ap()
    aps["out"] = nc.dram_tensor("out_0", (1, SEQ, D), F32, kind="ExternalOutput").ap()
    hybrid_backbone(nc, aps)
    result = run_bass_kernel_spmd(nc, [arrays], core_ids=[0])
    return result.results[0]["out_0"]
```
